# Optimizing a Trainium2 kernel written in Bass

```python
import jax, jax.numpy as jnp
from jax import lax
import numpy as np
import math
import jax
import jax.numpy as jnp

D_MODEL = 1024
BATCH = 1
SEQ = 512
DEPTH = 2

N_MIXERS = 2
BLOCK_Q = 128
EPS = 1e-6
FOX_HEADS = 16
FOX_HEAD_DIM = D_MODEL // FOX_HEADS
FOX_IN = 3 * D_MODEL + FOX_HEADS
FORGET_BIAS_INIT = 3.0
MLA_HEADS = 16
MLA_Q_RANK = 384
MLA_KV_RANK = 256
MLA_NOPE_DIM = 64
MLA_ROPE_DIM = 32
MLA_V_DIM = 64
MLA_QK_DIM = MLA_NOPE_DIM + MLA_ROPE_DIM
MLA_IN = MLA_Q_RANK + MLA_KV_RANK + MLA_ROPE_DIM
ROPE_THETA = 10000.0
N_GROUPS = 4
EXPERTS_PER_GROUP = 4
N_EXPERTS = N_GROUPS * EXPERTS_PER_GROUP
TOP_K_IN_GROUP = 2
D_EXPERT = 256

N_FOX_LAYERS = (DEPTH + 1) // 2
N_MLA_LAYERS = DEPTH // 2


def rmsnorm(x, g):
    xf = x.astype(jnp.float32)
    y = xf * lax.rsqrt(jnp.mean(xf * xf, axis=-1, keepdims=True) + EPS)
    return (y * g.astype(jnp.float32)).astype(x.dtype)

def rope(x, positions):
    half = MLA_ROPE_DIM // 2
    inv_freq = ROPE_THETA ** (-jnp.arange(0, half, dtype=jnp.float32) / half)
    ang = positions.astype(jnp.float32)[..., None] * inv_freq
    cos = jnp.cos(ang)[:, :, None, :]
    sin = jnp.sin(ang)[:, :, None, :]
    xf = x.astype(jnp.float32)
    x1, x2 = xf[..., :half], xf[..., half:]
    out = jnp.concatenate([x1 * cos - x2 * sin, x1 * sin + x2 * cos], axis=-1)
    return out.astype(x.dtype)

def causal_block_attention(q, k, v, scale, cum=None):
    B, H, S, dk = q.shape
    nb = S // BLOCK_Q
    qb = q.reshape(B, H, nb, BLOCK_Q, dk).transpose(2, 0, 1, 3, 4)
    kpos = jnp.arange(S)

    def one_block(args):
        i, qi = args
        s = jnp.einsum('bhqd,bhkd->bhqk', qi, k).astype(jnp.float32) * scale
        if cum is not None:
            ci = lax.dynamic_slice_in_dim(cum, i * BLOCK_Q, BLOCK_Q, axis=2)
            s = s + ci[..., :, None] - cum[..., None, :]
        qpos = i * BLOCK_Q + jnp.arange(BLOCK_Q)
        mask = kpos[None, :] <= qpos[:, None]
        s = jnp.where(mask, s, -jnp.inf)
        p = jax.nn.softmax(s, axis=-1)
        return jnp.einsum('bhqk,bhkd->bhqd', p.astype(v.dtype), v)

    o = lax.map(one_block, (jnp.arange(nb), qb))
    return o.transpose(1, 2, 0, 3, 4).reshape(B, H, S, v.shape[-1])

def fox_mixer(h, w_in, b_f, q_norm, k_norm, w_out):
    B, S, D = h.shape
    proj = h @ w_in
    q = proj[..., :D].reshape(B, S, FOX_HEADS, FOX_HEAD_DIM)
    k = proj[..., D:2 * D].reshape(B, S, FOX_HEADS, FOX_HEAD_DIM)
    v = proj[..., 2 * D:3 * D].reshape(B, S, FOX_HEADS, FOX_HEAD_DIM)
    f_logit = proj[..., 3 * D:]
    q = rmsnorm(q, q_norm)
    k = rmsnorm(k, k_norm)
    log_f = jax.nn.log_sigmoid((f_logit + b_f).astype(jnp.float32))
    cum = jnp.cumsum(log_f, axis=1).transpose(0, 2, 1)
    o = causal_block_attention(q.transpose(0, 2, 1, 3), k.transpose(0, 2, 1, 3),
                               v.transpose(0, 2, 1, 3), FOX_HEAD_DIM ** -0.5, cum)
    o = o.transpose(0, 2, 1, 3).reshape(B, S, D)
    return o @ w_out

def mla_mixer(h, positions, w_in, q_lat_norm, kv_lat_norm, w_uq, w_ukv, q_norm, k_norm, w_out):
    B, S, D = h.shape
    proj = h @ w_in
    cq = rmsnorm(proj[..., :MLA_Q_RANK], q_lat_norm)
    ckv = rmsnorm(proj[..., MLA_Q_RANK:MLA_Q_RANK + MLA_KV_RANK], kv_lat_norm)
    k_rope = proj[..., MLA_Q_RANK + MLA_KV_RANK:]
    q = (cq @ w_uq).reshape(B, S, MLA_HEADS, MLA_QK_DIM)
    kv = (ckv @ w_ukv).reshape(B, S, MLA_HEADS, MLA_NOPE_DIM + MLA_V_DIM)
    k_nope, v = kv[..., :MLA_NOPE_DIM], kv[..., MLA_NOPE_DIM:]
    k = jnp.concatenate(
        [k_nope, jnp.broadcast_to(k_rope[:, :, None, :], (B, S, MLA_HEADS, MLA_ROPE_DIM))], axis=-1)
    q = rmsnorm(q, q_norm)
    k = rmsnorm(k, k_norm)
    q = jnp.concatenate([q[..., :MLA_NOPE_DIM], rope(q[..., MLA_NOPE_DIM:], positions)], axis=-1)
    k = jnp.concatenate([k[..., :MLA_NOPE_DIM], rope(k[..., MLA_NOPE_DIM:], positions)], axis=-1)
    o = causal_block_attention(q.transpose(0, 2, 1, 3), k.transpose(0, 2, 1, 3),
                               v.transpose(0, 2, 1, 3), MLA_QK_DIM ** -0.5)
    o = o.transpose(0, 2, 1, 3).reshape(B, S, MLA_HEADS * MLA_V_DIM)
    return o @ w_out

def hier_moe(h, w_grp, b_grp, w_rt, b_rt, w_gate, w_up, w_down):
    B, S, D = h.shape
    T = B * S
    t = h.reshape(T, D)
    g_logits = (t @ w_grp).astype(jnp.float32) + b_grp.astype(jnp.float32)
    g_prob = jax.nn.softmax(g_logits, axis=-1)
    g_top, g_idx = lax.top_k(g_prob, 1)
    e_logits = ((t @ w_rt).astype(jnp.float32) + b_rt.astype(jnp.float32)).reshape(
        T, N_GROUPS, EXPERTS_PER_GROUP)
    sel = jnp.broadcast_to(g_idx[:, :, None], (T, 1, EXPERTS_PER_GROUP))
    in_group = jnp.take_along_axis(e_logits, sel, axis=1)[:, 0]
    e_top, e_idx = lax.top_k(in_group, TOP_K_IN_GROUP)
    w = jax.nn.softmax(e_top, axis=-1) * g_top
    expert_id = g_idx * EXPERTS_PER_GROUP + e_idx
    combine = jnp.sum(jax.nn.one_hot(expert_id, N_EXPERTS, dtype=jnp.float32) * w[..., None], axis=1)
    a = jnp.einsum('td,edf->tef', t, w_gate)
    u = jnp.einsum('td,edf->tef', t, w_up)
    hidden = jax.nn.silu(a) * u * combine[..., None].astype(t.dtype)
    out = jnp.einsum('tef,efd->td', hidden, w_down)
    return out.reshape(B, S, D)

def first_inputs(seed: int = 0) -> dict:
    key = jax.random.key(seed)
    ks = jax.random.split(key, 32)
    D = D_MODEL
    nrm = lambda k, shape, scale: jax.random.normal(k, shape, jnp.float32) * scale
    gain = lambda k, shape: 1.0 + 0.02 * jax.random.normal(k, shape, jnp.float32)
    offsets = jax.random.randint(ks[2], (BATCH, 1), 0, 1024, dtype=jnp.int32)
    return {
        "x": nrm(ks[0], (BATCH, SEQ, D), 1.0),
        "c": nrm(ks[1], (BATCH, D), 1.0),
        "positions": offsets + jnp.arange(SEQ, dtype=jnp.int32)[None, :],
        "w_ada": nrm(ks[3], (DEPTH, D, 6 * D), 0.5 * D ** -0.5),
        "b_ada": nrm(ks[4], (DEPTH, 6 * D), 0.01),
        "mix_norm": gain(ks[5], (DEPTH, D)),
        "ffn_norm": gain(ks[6], (DEPTH, D)),
        "fox_w_in": nrm(ks[7], (N_FOX_LAYERS, D, FOX_IN), D ** -0.5),
        "fox_b_f": FORGET_BIAS_INIT + nrm(ks[8], (N_FOX_LAYERS, FOX_HEADS), 0.5),
        "fox_q_norm": gain(ks[9], (N_FOX_LAYERS, FOX_HEAD_DIM)),
        "fox_k_norm": gain(ks[10], (N_FOX_LAYERS, FOX_HEAD_DIM)),
        "fox_w_out": nrm(ks[11], (N_FOX_LAYERS, D, D), D ** -0.5),
        "mla_w_in": nrm(ks[12], (N_MLA_LAYERS, D, MLA_IN), D ** -0.5),
        "mla_q_lat_norm": gain(ks[13], (N_MLA_LAYERS, MLA_Q_RANK)),
        "mla_kv_lat_norm": gain(ks[14], (N_MLA_LAYERS, MLA_KV_RANK)),
        "mla_w_uq": nrm(ks[15], (N_MLA_LAYERS, MLA_Q_RANK, MLA_HEADS * MLA_QK_DIM), MLA_Q_RANK ** -0.5),
        "mla_w_ukv": nrm(ks[16], (N_MLA_LAYERS, MLA_KV_RANK, MLA_HEADS * (MLA_NOPE_DIM + MLA_V_DIM)),
                         MLA_KV_RANK ** -0.5),
        "mla_q_norm": gain(ks[17], (N_MLA_LAYERS, MLA_QK_DIM)),
        "mla_k_norm": gain(ks[18], (N_MLA_LAYERS, MLA_QK_DIM)),
        "mla_w_out": nrm(ks[19], (N_MLA_LAYERS, MLA_HEADS * MLA_V_DIM, D), (MLA_HEADS * MLA_V_DIM) ** -0.5),
        "moe_w_grp": nrm(ks[20], (DEPTH, D, N_GROUPS), D ** -0.5),
        "moe_b_grp": nrm(ks[21], (DEPTH, N_GROUPS), 0.01),
        "moe_w_rt": nrm(ks[22], (DEPTH, D, N_EXPERTS), D ** -0.5),
        "moe_b_rt": nrm(ks[23], (DEPTH, N_EXPERTS), 0.01),
        "moe_w_gate": nrm(ks[24], (DEPTH, N_EXPERTS, D, D_EXPERT), D ** -0.5),
        "moe_w_up": nrm(ks[25], (DEPTH, N_EXPERTS, D, D_EXPERT), D ** -0.5),
        "moe_w_down": nrm(ks[26], (DEPTH, N_EXPERTS, D_EXPERT, D), D_EXPERT ** -0.5),
    }

def first_block(x, c, positions, w_ada, b_ada, mix_norm, ffn_norm,
              fox_w_in, fox_b_f, fox_q_norm, fox_k_norm, fox_w_out,
              mla_w_in, mla_q_lat_norm, mla_kv_lat_norm, mla_w_uq, mla_w_ukv, mla_q_norm, mla_k_norm,
              mla_w_out,
              moe_w_grp, moe_b_grp, moe_w_rt, moe_b_rt, moe_w_gate, moe_w_up, moe_w_down):
    c_act = jax.nn.silu(c)
    for i in range(DEPTH):
        mod = c_act @ w_ada[i] + b_ada[i]
        sh1, sc1, g1, sh2, sc2, g2 = [m[:, None, :] for m in jnp.split(mod, 6, axis=-1)]
        h = rmsnorm(x, mix_norm[i]) * (1.0 + sc1) + sh1
        j = i // N_MIXERS
        if i % N_MIXERS == 0:
            y = fox_mixer(h, fox_w_in[j], fox_b_f[j], fox_q_norm[j], fox_k_norm[j], fox_w_out[j])
        else:
            y = mla_mixer(h, positions, mla_w_in[j], mla_q_lat_norm[j], mla_kv_lat_norm[j],
                          mla_w_uq[j], mla_w_ukv[j], mla_q_norm[j], mla_k_norm[j], mla_w_out[j])
        x = x + g1 * y
        h = rmsnorm(x, ffn_norm[i]) * (1.0 + sc2) + sh2
        x = x + g2 * hier_moe(h, moe_w_grp[i], moe_b_grp[i], moe_w_rt[i], moe_b_rt[i],
                              moe_w_gate[i], moe_w_up[i], moe_w_down[i])
    return x


F32 = jnp.float32
N_MIXERS_2 = 4
N_META = 16
EXPAND = 2
D_INNER = EXPAND * D_MODEL
RMS_EPS = 1e-6
LN_EPS = 1e-5
Q_BLOCK = 128

HY_SHORT = 3
HY_EMB = 33
HY_BANDS = (HY_EMB - 1) // 2
HY_HIDDEN = 64
HY_SHORT_DECAY_PCT = 0.3
HY_LONG_DECAY_PCT = 1.5
HY_DECAY_TARGET = 1e-2
HY_FILTER_EPS = 1e-6

DA_HEAD_DIM = 64
DA_V_DIM = 2 * DA_HEAD_DIM
DA_HEADS = D_INNER // DA_V_DIM
DA_QK = DA_HEADS * 2 * DA_HEAD_DIM
DA_NORM_EPS = 1e-5

GDN_HEAD_DIM = 128
GDN_V_HEADS = D_INNER // GDN_HEAD_DIM
GDN_K_HEADS = GDN_V_HEADS // 2
GDN_QK = GDN_K_HEADS * GDN_HEAD_DIM
GDN_SHORT = 3
GDN_CHUNK = 64

CF_WIDTH = 31

N_A = (DEPTH + 3) // N_MIXERS_2
N_B = (DEPTH + 2) // N_MIXERS_2
N_C = (DEPTH + 1) // N_MIXERS_2
N_D = DEPTH // N_MIXERS_2


def rmsnorm_2(x, g, eps=RMS_EPS):
    xf = x.astype(F32)
    y = xf * lax.rsqrt(jnp.mean(xf * xf, axis=-1, keepdims=True) + eps)
    return (y * g.astype(F32)).astype(x.dtype)

def layernorm(x, g, b, eps=LN_EPS):
    xf = x.astype(F32)
    mu = jnp.mean(xf, axis=-1, keepdims=True)
    var = jnp.mean(jnp.square(xf - mu), axis=-1, keepdims=True)
    y = (xf - mu) * lax.rsqrt(var + eps)
    return (y * g.astype(F32) + b.astype(F32)).astype(x.dtype)

def l2norm(x, eps=1e-6):
    xf = x.astype(F32)
    return xf * lax.rsqrt(jnp.sum(xf * xf, axis=-1, keepdims=True) + eps)

def dwconv_centred(x, w, b=None):
    width, ch = w.shape
    y = lax.conv_general_dilated(
        x, w[:, None, :].astype(x.dtype), window_strides=(1,),
        padding=[(width // 2, width // 2)],
        dimension_numbers=("NWC", "WIO", "NWC"), feature_group_count=ch)
    if b is not None:
        y = y + b.astype(x.dtype)
    return y

def rope_tables(T, dim):
    inv_freq = ROPE_THETA ** (-jnp.arange(0, dim, 2, dtype=F32) / dim)
    ang = jnp.arange(T, dtype=F32)[:, None] * inv_freq[None, :]
    return jnp.cos(ang), jnp.sin(ang)

def apply_rope(x, cos, sin):
    half = x.shape[-1] // 2
    xf = x.astype(F32)
    x1, x2 = xf[..., :half], xf[..., half:]
    c = cos[None, :, None, None, :]
    s = sin[None, :, None, None, :]
    return jnp.concatenate([x1 * c - x2 * s, x2 * c + x1 * s], axis=-1).astype(x.dtype)

def hyena_filters(T, w1, b1, w2, b2, w3, b3, w4, freq):
    t = jnp.linspace(0.0, 1.0, T, dtype=F32)[:, None]
    w = 2.0 * math.pi * jnp.arange(T, dtype=F32)[:, None] / T
    bands = jnp.linspace(1e-4, HY_BANDS - 1, HY_BANDS, dtype=F32)[None, :]
    z = jnp.concatenate([t, jnp.cos(bands * w), -jnp.sin(bands * w)], axis=-1)
    fr = freq.astype(F32)
    hdn = jnp.sin(fr * (z @ w1.astype(F32) + b1.astype(F32)))
    hdn = jnp.sin(fr * (hdn @ w2.astype(F32) + b2.astype(F32)))
    hdn = jnp.sin(fr * (hdn @ w3.astype(F32) + b3.astype(F32)))
    filt = (hdn @ w4.astype(F32)).reshape(T, 2, D_INNER)
    max_decay = math.log(HY_DECAY_TARGET) / HY_SHORT_DECAY_PCT
    min_decay = math.log(HY_DECAY_TARGET) / HY_LONG_DECAY_PCT
    deltas = jnp.abs(jnp.linspace(min_decay, max_decay, D_INNER, dtype=F32))
    filt = filt * jnp.exp(-t * deltas[None, :])[:, None, :]
    filt = filt / (jnp.sum(jnp.abs(filt), axis=(0, 1), keepdims=True) + HY_FILTER_EPS)
    return filt[:, 0], filt[:, 1]

def bidir_long_conv(v, h_fwd, h_bwd, skip):
    T = v.shape[1]
    n = 2 * T
    taps = jnp.concatenate(
        [h_fwd, jnp.zeros((1, h_fwd.shape[1]), F32), h_bwd[:0:-1]], axis=0)
    vf = v.astype(F32)
    y = jnp.fft.irfft(jnp.fft.rfft(vf, n=n, axis=1) * jnp.fft.rfft(taps, n=n, axis=0)[None],
                      n=n, axis=1)[:, :T]
    return (y + vf * skip.astype(F32)).astype(v.dtype)

def hyena_mixer(h, w_in, b_in, conv_w, conv_b, f_w1, f_b1, f_w2, f_b2, f_w3, f_b3, f_w4,
                f_freq, skip, w_out):
    T = h.shape[1]
    u = h @ w_in + b_in
    streams = dwconv_centred(u[..., :3 * D_INNER], conv_w, conv_b)
    x0, x1, v = jnp.split(streams, 3, axis=-1)
    z = u[..., 3 * D_INNER:]
    h_fwd, h_bwd = hyena_filters(T, f_w1, f_b1, f_w2, f_b2, f_w3, f_b3, f_w4, f_freq)
    v = bidir_long_conv(v * x1, h_fwd, h_bwd, skip)
    y = v * x0
    return (y * jax.nn.silu(z)) @ w_out

def diff_attention_mixer(h, w_in, lam_vecs, subln, w_out, cos, sin, layer_idx):
    B, T, _ = h.shape
    u = h @ w_in
    q = u[..., :DA_QK].reshape(B, T, DA_HEADS, 2, DA_HEAD_DIM)
    k = u[..., DA_QK:2 * DA_QK].reshape(B, T, DA_HEADS, 2, DA_HEAD_DIM)
    v = u[..., 2 * DA_QK:2 * DA_QK + D_INNER].reshape(B, T, DA_HEADS, DA_V_DIM)
    z = u[..., 2 * DA_QK + D_INNER:]
    q = apply_rope(q, cos, sin)
    k = apply_rope(k, cos, sin)
    lam_init = 0.8 - 0.6 * math.exp(-0.3 * layer_idx)
    lv = lam_vecs.astype(F32)
    lam = jnp.exp(jnp.sum(lv[0] * lv[1])) - jnp.exp(jnp.sum(lv[2] * lv[3])) + lam_init
    scale = DA_HEAD_DIM ** -0.5
    n_blk = -(-T // Q_BLOCK)
    q = jnp.pad(q, ((0, 0), (0, n_blk * Q_BLOCK - T), (0, 0), (0, 0), (0, 0)))
    q_blocks = q.reshape(B, n_blk, Q_BLOCK, DA_HEADS, 2, DA_HEAD_DIM).swapaxes(0, 1)

    def attend(qb):
        s = jnp.einsum("bqhmd,bkhmd->bhmqk", qb, k).astype(F32) * scale
        p = jax.nn.softmax(s, axis=-1)
        p = p[:, :, 0] - lam * p[:, :, 1]
        return jnp.einsum("bhqk,bkhd->bqhd", p.astype(v.dtype), v)

    o = lax.map(attend, q_blocks)
    o = o.swapaxes(0, 1).reshape(B, n_blk * Q_BLOCK, DA_HEADS, DA_V_DIM)[:, :T]
    o = rmsnorm_2(o, subln, DA_NORM_EPS) * (1.0 - lam_init)
    return (o.reshape(B, T, D_INNER) * jax.nn.silu(z)) @ w_out

def chunk_gated_delta(q, k, v, g, beta):
    B, Tp, H, dk = q.shape
    dv = v.shape[-1]
    C = GDN_CHUNK
    n = Tp // C

    def to_chunks(a):
        return a.reshape(B, n, C, H, -1).transpose(0, 3, 1, 2, 4)

    q, k, v = to_chunks(q), to_chunks(k), to_chunks(v)
    beta = to_chunks(beta[..., None])
    g = jnp.cumsum(to_chunks(g[..., None])[..., 0], axis=-1)
    idx = jnp.arange(C)
    strict = idx[:, None] > idx[None, :]
    incl = idx[:, None] >= idx[None, :]
    gdiff = g[..., :, None] - g[..., None, :]
    k_beta = k * beta
    a_mat = jnp.einsum("bhncd,bhnsd->bhncs", k_beta, k) * jnp.exp(jnp.where(strict, gdiff, -jnp.inf))
    rhs = jnp.concatenate([v * beta, k_beta * jnp.exp(g)[..., None]], axis=-1)
    sol = lax.linalg.triangular_solve(a_mat + jnp.eye(C, dtype=F32), rhs,
                                      left_side=True, lower=True)
    u_vals, w_vals = sol[..., :dv], sol[..., dv:]
    attn_intra = jnp.einsum("bhncd,bhnsd->bhncs", q, k) * jnp.exp(jnp.where(incl, gdiff, -jnp.inf))
    q_dec = q * jnp.exp(g)[..., None]
    g_last = g[..., -1]
    k_end = k * jnp.exp(g_last[..., None] - g)[..., None]

    def step(S, xs):
        qd, ke, uc, wc, ac, gl = xs
        v_new = uc - jnp.einsum("bhcd,bhde->bhce", wc, S)
        o = jnp.einsum("bhcd,bhde->bhce", qd, S) + jnp.einsum("bhcs,bhse->bhce", ac, v_new)
        S = S * jnp.exp(gl)[..., None, None] + jnp.einsum("bhcd,bhce->bhde", ke, v_new)
        return S, o

    xs = tuple(jnp.moveaxis(a, 2, 0) for a in (q_dec, k_end, u_vals, w_vals, attn_intra, g_last))
    S0 = jnp.zeros((B, H, dk, dv), F32)
    _, o = lax.scan(step, S0, xs)
    return o.transpose(1, 0, 3, 2, 4).reshape(B, Tp, H, dv)

def gdn_mixer(h, w_in, conv_w, a_log, dt_bias, o_norm, w_out):
    B, T, _ = h.shape
    u = h @ w_in
    n_qkv = 2 * GDN_QK + D_INNER
    qkv = jax.nn.silu(dwconv_centred(u[..., :n_qkv], conv_w))
    z = u[..., n_qkv:n_qkv + D_INNER].reshape(B, T, GDN_V_HEADS, GDN_HEAD_DIM)
    ab = u[..., n_qkv + D_INNER:].astype(F32).reshape(B, T, 2, 2, GDN_V_HEADS)
    q = l2norm(qkv[..., :GDN_QK].reshape(B, T, GDN_K_HEADS, GDN_HEAD_DIM)) * GDN_HEAD_DIM ** -0.5
    k = l2norm(qkv[..., GDN_QK:2 * GDN_QK].reshape(B, T, GDN_K_HEADS, GDN_HEAD_DIM))
    v = qkv[..., 2 * GDN_QK:].astype(F32).reshape(B, T, GDN_V_HEADS, GDN_HEAD_DIM)
    rep = GDN_V_HEADS // GDN_K_HEADS
    q = jnp.repeat(q, rep, axis=2)
    k = jnp.repeat(k, rep, axis=2)
    g = -jnp.exp(a_log.astype(F32)) * jax.nn.softplus(ab[:, :, 0] + dt_bias.astype(F32))
    beta = jax.nn.sigmoid(ab[:, :, 1])
    pad_front = (-N_META) % GDN_CHUNK
    pad_end = (-(T - N_META)) % GDN_CHUNK

    def padt(a):
        return jnp.pad(a, [(0, 0), (pad_front, pad_end)] + [(0, 0)] * (a.ndim - 2))

    q, k, v, g, beta = padt(q), padt(k), padt(v), padt(g), padt(beta)

    def rev(a):
        return jnp.flip(a, axis=1)

    o_fwd = chunk_gated_delta(q, k, v, g[:, :, 0], beta[:, :, 0])
    o_bwd = rev(chunk_gated_delta(rev(q), rev(k), rev(v), rev(g[:, :, 1]), rev(beta[:, :, 1])))
    o = (o_fwd + o_bwd)[:, pad_front:pad_front + T].astype(h.dtype)
    o = rmsnorm_2(o, o_norm) * jax.nn.silu(z)
    return o.reshape(B, T, D_INNER) @ w_out

def conformer_conv_mixer(h, w_in, b_in, dw_w, dw_b, ln_g, ln_b, w_out, b_out):
    u = h @ w_in + b_in
    a, a_gate, z = jnp.split(u, 3, axis=-1)
    y = a * jax.nn.sigmoid(a_gate)
    y = dwconv_centred(y, dw_w, dw_b)
    y = jax.nn.silu(layernorm(y, ln_g, ln_b))
    return (y * jax.nn.silu(z)) @ w_out + b_out

def second_inputs(seed: int = 0) -> dict:
    key = jax.random.key(seed)
    ks = jax.random.split(key, 48)
    counter = [0]

    def nk():
        counter[0] += 1
        return ks[counter[0] - 1]

    def nrm(shape, scale):
        return jax.random.normal(nk(), shape, F32) * scale

    def gain(shape):
        return 1.0 + nrm(shape, 0.02)

    E = D_INNER
    dt = jnp.exp(jax.random.uniform(nk(), (N_C, 2, GDN_V_HEADS), F32, math.log(1e-3), math.log(1e-1)))
    a_log = jnp.log(jax.random.uniform(nk(), (N_C, 2, GDN_V_HEADS), F32, 1.0, 16.0))
    return {
        "x": nrm((BATCH, SEQ, D_MODEL), 1.0),
        "meta": nrm((N_META, D_MODEL), 1.0),
        "norm_pre": gain((DEPTH, D_MODEL)),
        "norm_post": gain((DEPTH, D_MODEL)),
        "hy_w_in": nrm((N_A, D_MODEL, 4 * E), D_MODEL ** -0.5),
        "hy_b_in": nrm((N_A, 4 * E), 0.02),
        "hy_conv_w": nrm((N_A, HY_SHORT, 3 * E), HY_SHORT ** -0.5),
        "hy_conv_b": nrm((N_A, 3 * E), 0.02),
        "hy_f_w1": nrm((N_A, HY_EMB, HY_HIDDEN), HY_EMB ** -0.5),
        "hy_f_b1": nrm((N_A, HY_HIDDEN), 0.02),
        "hy_f_w2": nrm((N_A, HY_HIDDEN, HY_HIDDEN), HY_HIDDEN ** -0.5),
        "hy_f_b2": nrm((N_A, HY_HIDDEN), 0.02),
        "hy_f_w3": nrm((N_A, HY_HIDDEN, HY_HIDDEN), HY_HIDDEN ** -0.5),
        "hy_f_b3": nrm((N_A, HY_HIDDEN), 0.02),
        "hy_f_w4": nrm((N_A, HY_HIDDEN, 2 * E), HY_HIDDEN ** -0.5),
        "hy_f_freq": gain((N_A, HY_HIDDEN)),
        "hy_skip": nrm((N_A, E), 1.0),
        "hy_w_out": nrm((N_A, E, D_MODEL), E ** -0.5),
        "da_w_in": nrm((N_B, D_MODEL, 2 * DA_QK + 2 * E), D_MODEL ** -0.5),
        "da_lambda": nrm((N_B, 4, DA_HEAD_DIM), 0.1),
        "da_subln": gain((N_B, DA_V_DIM)),
        "da_w_out": nrm((N_B, E, D_MODEL), E ** -0.5),
        "gdn_w_in": nrm((N_C, D_MODEL, 2 * GDN_QK + 2 * E + 4 * GDN_V_HEADS), D_MODEL ** -0.5),
        "gdn_conv_w": nrm((N_C, GDN_SHORT, 2 * GDN_QK + E), GDN_SHORT ** -0.5),
        "gdn_a_log": a_log,
        "gdn_dt_bias": dt + jnp.log(-jnp.expm1(-dt)),
        "gdn_o_norm": gain((N_C, GDN_HEAD_DIM)),
        "gdn_w_out": nrm((N_C, E, D_MODEL), E ** -0.5),
        "cf_w_in": nrm((N_D, D_MODEL, 3 * E), D_MODEL ** -0.5),
        "cf_b_in": nrm((N_D, 3 * E), 0.02),
        "cf_dw_w": nrm((N_D, CF_WIDTH, E), CF_WIDTH ** -0.5),
        "cf_dw_b": nrm((N_D, E), 0.02),
        "cf_ln_g": gain((N_D, E)),
        "cf_ln_b": nrm((N_D, E), 0.02),
        "cf_w_out": nrm((N_D, E, D_MODEL), E ** -0.5),
        "cf_b_out": nrm((N_D, D_MODEL), 0.02),
    }

def second_block(x, meta, norm_pre, norm_post,
              hy_w_in, hy_b_in, hy_conv_w, hy_conv_b, hy_f_w1, hy_f_b1, hy_f_w2, hy_f_b2,
              hy_f_w3, hy_f_b3, hy_f_w4, hy_f_freq, hy_skip, hy_w_out,
              da_w_in, da_lambda, da_subln, da_w_out,
              gdn_w_in, gdn_conv_w, gdn_a_log, gdn_dt_bias, gdn_o_norm, gdn_w_out,
              cf_w_in, cf_b_in, cf_dw_w, cf_dw_b, cf_ln_g, cf_ln_b, cf_w_out, cf_b_out):
    B = x.shape[0]
    h = jnp.concatenate(
        [jnp.broadcast_to(meta[None].astype(x.dtype), (B, N_META, D_MODEL)), x], axis=1)
    T = h.shape[1]
    cos, sin = rope_tables(T, DA_HEAD_DIM)
    for i in range(DEPTH):
        m, j = i % N_MIXERS_2, i // N_MIXERS_2
        y = rmsnorm_2(h, norm_pre[i])
        if m == 0:
            y = hyena_mixer(y, hy_w_in[j], hy_b_in[j], hy_conv_w[j], hy_conv_b[j],
                            hy_f_w1[j], hy_f_b1[j], hy_f_w2[j], hy_f_b2[j], hy_f_w3[j], hy_f_b3[j],
                            hy_f_w4[j], hy_f_freq[j], hy_skip[j], hy_w_out[j])
        elif m == 1:
            y = diff_attention_mixer(y, da_w_in[j], da_lambda[j], da_subln[j], da_w_out[j],
                                     cos, sin, i)
        elif m == 2:
            y = gdn_mixer(y, gdn_w_in[j], gdn_conv_w[j], gdn_a_log[j], gdn_dt_bias[j],
                          gdn_o_norm[j], gdn_w_out[j])
        else:
            y = conformer_conv_mixer(y, cf_w_in[j], cf_b_in[j], cf_dw_w[j], cf_dw_b[j],
                                     cf_ln_g[j], cf_ln_b[j], cf_w_out[j], cf_b_out[j])
        h = h + rmsnorm_2(y, norm_post[i])
    return h[:, N_META:]


def setup_inputs(seed=0):
    out = dict(first_inputs(seed))
    for name, value in second_inputs(seed + 1).items():
        if name != "x":
            out[name + "_2"] = value
    return out


def reference(
    x, c, positions, w_ada, b_ada, mix_norm, ffn_norm, fox_w_in, fox_b_f, fox_q_norm,
    fox_k_norm, fox_w_out, mla_w_in, mla_q_lat_norm, mla_kv_lat_norm, mla_w_uq, mla_w_ukv,
    mla_q_norm, mla_k_norm, mla_w_out, moe_w_grp, moe_b_grp, moe_w_rt, moe_b_rt, moe_w_gate,
    moe_w_up, moe_w_down, meta_2, norm_pre_2, norm_post_2, hy_w_in_2, hy_b_in_2, hy_conv_w_2,
    hy_conv_b_2, hy_f_w1_2, hy_f_b1_2, hy_f_w2_2, hy_f_b2_2, hy_f_w3_2, hy_f_b3_2, hy_f_w4_2,
    hy_f_freq_2, hy_skip_2, hy_w_out_2, da_w_in_2, da_lambda_2, da_subln_2, da_w_out_2,
    gdn_w_in_2, gdn_conv_w_2, gdn_a_log_2, gdn_dt_bias_2, gdn_o_norm_2, gdn_w_out_2, cf_w_in_2,
    cf_b_in_2, cf_dw_w_2, cf_dw_b_2, cf_ln_g_2, cf_ln_b_2, cf_w_out_2, cf_b_out_2,
):
    x = first_block(
        x, c, positions, w_ada, b_ada, mix_norm, ffn_norm, fox_w_in, fox_b_f, fox_q_norm,
        fox_k_norm, fox_w_out, mla_w_in, mla_q_lat_norm, mla_kv_lat_norm, mla_w_uq, mla_w_ukv,
        mla_q_norm, mla_k_norm, mla_w_out, moe_w_grp, moe_b_grp, moe_w_rt, moe_b_rt, moe_w_gate,
        moe_w_up, moe_w_down,
    )
    return second_block(
        x, meta_2, norm_pre_2, norm_post_2, hy_w_in_2, hy_b_in_2, hy_conv_w_2, hy_conv_b_2,
        hy_f_w1_2, hy_f_b1_2, hy_f_w2_2, hy_f_b2_2, hy_f_w3_2, hy_f_b3_2, hy_f_w4_2,
        hy_f_freq_2, hy_skip_2, hy_w_out_2, da_w_in_2, da_lambda_2, da_subln_2, da_w_out_2,
        gdn_w_in_2, gdn_conv_w_2, gdn_a_log_2, gdn_dt_bias_2, gdn_o_norm_2, gdn_w_out_2,
        cf_w_in_2, cf_b_in_2, cf_dw_w_2, cf_dw_b_2, cf_ln_g_2, cf_ln_b_2, cf_w_out_2,
        cf_b_out_2,
    )


_drawn_inputs = setup_inputs


def setup_inputs(seed=0):
    import zlib

    import numpy as np

    out = dict(_drawn_inputs(seed))
    spreads = {}
    factors = {'mix_norm': 4.005,
     'fox_q_norm': 4.331,
     'fox_k_norm': 4.055,
     'mla_q_lat_norm': 8.0,
     'mla_kv_lat_norm': 4.798,
     'mla_q_norm': 8.0,
     'mla_k_norm': 6.842,
     'moe_b_grp': 4.684,
     'moe_b_rt': 5.49,
     'norm_post_2': 2.723,
     'hy_f_b1_2': 8.0,
     'hy_f_b2_2': 8.0,
     'hy_f_b3_2': 8.0,
     'hy_f_freq_2': 8.0,
     'da_subln_2': 5.706}
    for name, (base, spread) in spreads.items():
        noise = np.random.default_rng([zlib.crc32(name.encode()), seed]).standard_normal(out[name].shape)
        drawn = base * np.exp(spread * noise) if base else spread * noise
        out[name] = jnp.asarray(drawn.astype(out[name].dtype))
    for name, factor in factors.items():
        out[name] = (out[name] * factor).astype(out[name].dtype)
    return out
```

```python
from contextlib import ExitStack

import numpy as np

import concourse.bass as bass
from concourse import mybir

F32 = mybir.dt.float32
F32R = mybir.dt.float32r
I32 = mybir.dt.int32
ALU = mybir.AluOpType
ACT = mybir.ActivationFunctionType
AX_X = mybir.AxisListType.X
AX_XY = mybir.AxisListType.XY

P = 128
D = 1024
KD = D // P
META = 16
SEQ = 512
T = META + SEQ
HALF = T // 2
TQ = 106
NQ = 5
QS = [min(TQ, T - TQ * i) for i in range(NQ)]
LAYERS = 2
EPS = 1e-6
NEG = -1e30
PI_IN = 3.1415925
TWO_PI_1 = 6.28125
TWO_PI_2 = float(np.float32(np.round((2 * np.pi - 6.28125) * 2**21) / 2**21))
TWO_PI_3 = float(2 * np.pi - TWO_PI_1 - TWO_PI_2)
ROUND = 12582912.0

FOX_H, FOX_D = 16, 64
MLA_H, MLA_QK, MLA_NOPE = 16, 96, 64
KQ, KKV = 3, 2
E_N, E_G, E_PG, E_F = 16, 4, 4, 256
D_IN = 2048
HY_G = 8
FREQ = T + 1
HY_HID, HY_EMB = 64, 33
DA_H, DA_D = 16, 64
LAM_INIT = 0.8 - 0.6 * float(np.exp(-0.3 * 1))

CHUNK = 2048
RAW, SPLIT = 3, 2

C_ID, C_ONED, C_B64, C_O96, C_O384, C_O256, C_O128, C_MASK, C_R96, C_R128, C_ONE = (P * i for i in range(11))
C_WF = 11 * P
C_M0 = C_WF + NQ
C_INVF, C_SGN, C_EPS, C_EPS5, C_HPI, C_EPSL = (C_M0 + 1 + i for i in range(6))
C_N = C_EPSL + 1

V_C, V_MIX, V_FFN, V_PRE, V_POST, V_SKIP, V_QLAT, V_KVLAT = 0, 8, 24, 40, 56, 72, 88, 91
V_BADA, V_HYB, V_CB, V_CW, V_CW2 = 128, 256, 320, 384, 512
VEC_ROWS = [93, 96, 112, 96, 48]


def constants():
    c = np.zeros((P, C_N), np.float32)
    eye = np.eye(P, dtype=np.float32)
    c[:, C_ID:C_ID + P] = eye
    c[:, C_ONED:C_ONED + P] = 1.0 / D
    for b in range(2):
        c[64 * b:64 * b + 64, C_B64 + 64 * b:C_B64 + 64 * b + 64] = 1.0 / 64
    c[:96, C_O96:C_O96 + 96] = 1.0 / 96
    c[:, C_O384:C_O384 + P] = 1.0 / 384
    c[:, C_O256:C_O256 + P] = 1.0 / 256
    c[:, C_O128:C_O128 + P] = 1.0 / 128
    c[:, C_ONE:C_ONE + P] = 1.0
    c[:, C_MASK:C_MASK + P] = np.triu(np.full((P, P), NEG, np.float32), 1)
    r96 = np.zeros((P, P), np.float32)
    for i in range(16):
        r96[64 + i, 80 + i] = r96[80 + i, 64 + i] = 1.0
    c[:, C_R96:C_R96 + P] = r96
    r128 = np.zeros((P, P), np.float32)
    for b in (0, 64):
        for i in range(32):
            r128[b + i, b + 32 + i] = r128[b + 32 + i, b + i] = 1.0
    c[:, C_R128:C_R128 + P] = r128
    f = np.arange(NQ)[None, :] * TQ + np.arange(P)[:, None]
    w = np.where((f == 0) | (f == T), 1.0, 2.0) / (2 * T)
    c[:, C_WF:C_WF + NQ] = np.where((f < FREQ) & (np.arange(P)[:, None] < TQ), w, 0.0)
    c[:, C_M0] = 1.0
    c[0, C_M0] = 0.0
    inv = (10000.0 ** (-np.arange(16, dtype=np.float32) / 16)).astype(np.float32)
    c[64:80, C_INVF] = inv
    c[80:96, C_INVF] = inv
    c[64:80, C_SGN] = -1.0
    c[80:96, C_SGN] = 1.0
    c[:, C_EPS] = EPS
    c[:, C_EPS5] = 1e-5
    c[:, C_HPI] = np.pi / 2
    c[:, C_EPSL] = 1e-6
    t = np.arange(NQ * TQ)
    ang = (t[:, None] * t[None, :] % (2 * T)) * (np.pi / T)
    dft = np.stack([np.cos(ang), np.sin(ang)])
    dft[:, FREQ:, :] = 0.0
    dft[:, :, FREQ:] = 0.0
    dft = dft.reshape(2, NQ, TQ, NQ * TQ).transpose(2, 0, 1, 3).reshape(TQ, -1).astype(np.float32)
    inv = (np.float32(10000.0) ** (-np.arange(0, 64, 2, dtype=np.float32) / 64)).astype(np.float32)
    a = np.arange(T, dtype=np.float32)[None, :] * inv[:, None]
    co, si = np.cos(a), np.sin(a)
    rope = np.stack([np.concatenate([co] * 4), np.concatenate([-si, si] * 2)], 1).reshape(P, -1).astype(np.float32)
    tt = np.linspace(0.0, 1.0, T, dtype=np.float32)[:, None]
    ww = (2.0 * np.pi * np.arange(T, dtype=np.float32)[:, None] / T).astype(np.float32)
    bands = np.linspace(1e-4, 15, 16, dtype=np.float32)[None, :]
    feats = np.concatenate([tt, np.cos(bands * ww), -np.sin(bands * ww)], 1).T.astype(np.float32).copy()
    lo, hi = np.log(1e-2) / 1.5, np.log(1e-2) / 0.3
    deltas = np.abs(np.linspace(lo, hi, D_IN, dtype=np.float32))
    decay = np.exp(-tt * deltas[None, :]).astype(np.float32)
    return {"cst": c, "dft": dft, "rope": rope, "feats": feats, "decay": decay}


def build(nc, cc, out):
    with ExitStack() as ctx:
        def sb(name, shape, dt=F32):
            return ctx.enter_context(nc.sbuf_tensor(name, shape, dt))

        def sem(name):
            return ctx.enter_context(nc.semaphore(name))

        s_act_chain = sem("act_chain")
        s_dve_chain = sem("dve_chain")
        s_ada_pe = sem("ada_pe")
        s_ada_s = sem("ada_s")
        s_hyf_rd = sem("hyf_rd")
        s_ada_used = sem("ada_used")
        s_att_dg = sem("att_dg")
        s_att_ex = sem("att_ex")
        s_att_mx = sem("att_mx")
        s_att_of = sem("att_of")
        s_att_pt = sem("att_pt")
        s_att_pv = sem("att_pv")
        s_att_ri = sem("att_ri")
        s_att_s = sem("att_s")
        s_cact = sem("cact")
        s_cst_in = sem("cst_in")
        s_da_fe = sem("da_fe")
        s_da_cb = sem("da_cb")
        s_da_dg = sem("da_dg")
        s_da_ex = sem("da_ex")
        s_da_mx = sem("da_mx")
        s_da_o = sem("da_o")
        s_da_oh = sem("da_oh")
        s_da_ol = sem("da_ol")
        s_da_on = sem("da_on")
        s_da_oz = sem("da_oz")
        s_da_pa = sem("da_pa")
        s_da_pb = sem("da_pb")
        s_da_pt = sem("da_pt")
        s_da_pv = sem("da_pv")
        s_da_qf = sem("da_qf")
        s_da_rq = sem("da_rq")
        s_da_s = sem("da_s")
        s_da_sq = sem("da_sq")
        s_da_ss = sem("da_ss")
        s_da_t1 = sem("da_t1")
        s_fox_cum = sem("fox_cum")
        s_fox_f = sem("fox_f")
        s_fox_fz = sem("fox_fz")
        s_fox_ln = sem("fox_ln")
        s_fox_nb = sem("fox_nb")
        s_fox_qk = sem("fox_qk")
        s_fox_sq = sem("fox_sq")
        s_fox_ss = sem("fox_ss")
        s_hy_H = sem("hy_H")
        s_hy_a = sem("hy_a")
        s_hy_c = sem("hy_c")
        s_hy_cv = sem("hy_cv")
        s_hy_g = sem("hy_g")
        s_hy_i = sem("hy_i")
        s_hy_m = sem("hy_m")
        s_hy_p = sem("hy_p")
        s_hy_pad = sem("hy_pad")
        s_hy_t = sem("hy_t")
        s_hy_te = sem("hy_te")
        s_hy_u = sem("hy_u")
        s_hy_v = sem("hy_v")
        s_hy_w = sem("hy_w")
        s_hy_yg = sem("hy_yg")
        s_hy_yh = sem("hy_yh")
        s_hy_yl = sem("hy_yl")
        s_hy_z = sem("hy_z")
        s_hyf_tb = sem("hyf_tb")
        s_hyf_hi = sem("hyf_hi")
        s_hyf_lo = sem("hyf_lo")
        s_hyf_A = sem("hyf_A")
        s_hyf_F = sem("hyf_F")
        s_hyf_H = sem("hyf_H")
        s_hyf_a = sem("hyf_a")
        s_hyf_d = sem("hyf_d")
        s_hyf_e = sem("hyf_e")
        s_hyf_f = sem("hyf_f")
        s_hyf_h = sem("hyf_h")
        s_hyf_in = sem("hyf_in")
        s_hyf_l = sem("hyf_l")
        s_hyf_l1 = sem("hyf_l1")
        s_hyf_m = sem("hyf_m")
        s_hyf_sin = sem("hyf_sin")
        s_hyf_st = sem("hyf_st")
        s_lam_e = sem("lam_e")
        s_lam_s = sem("lam_s")
        s_lat_cp = sem("lat_cp")
        s_lat_hi = sem("lat_hi")
        s_lat_kr = sem("lat_kr")
        s_lat_lo = sem("lat_lo")
        s_lat_n = sem("lat_n")
        s_lat_rt = sem("lat_rt")
        s_lat_sq = sem("lat_sq")
        s_lat_ss = sem("lat_ss")
        s_mla_qf = sem("mla_qf")
        s_mla_qn = sem("mla_qn")
        s_mla_rq = sem("mla_rq")
        s_mla_sq = sem("mla_sq")
        s_mla_ss = sem("mla_ss")
        s_mla_t1 = sem("mla_t1")
        s_mod = sem("mod")
        s_moe_b = sem("moe_b")
        s_moe_bc = sem("moe_bc")
        s_moe_cb = sem("moe_cb")
        s_moe_ct = sem("moe_ct")
        s_moe_cts = sem("moe_cts")
        s_moe_hh = sem("moe_hh")
        s_moe_hl = sem("moe_hl")
        s_moe_lt = sem("moe_lt")
        s_moe_ls = sem("moe_ls")
        s_moe_lg = sem("moe_lg")
        s_moe_re = sem("moe_re")
        s_moe_rx = sem("moe_rx")
        s_moe_sg = sem("moe_sg")
        s_moe_t = sem("moe_t")
        s_moe_u = sem("moe_u")
        s_norm_h = sem("norm_h")
        s_norm_hi = sem("norm_hi")
        s_norm_lo = sem("norm_lo")
        s_norm_rt = sem("norm_rt")
        s_norm_sq = sem("norm_sq")
        s_norm_ss = sem("norm_ss")
        s_o_hi = sem("o_hi")
        s_o_lo = sem("o_lo")
        s_pos_in = sem("pos_in")
        s_post_rt = sem("post_rt")
        s_post_sq = sem("post_sq")
        s_post_ss = sem("post_ss")
        s_rope_r = sem("rope_r")
        s_rope_s = sem("rope_s")
        s_rope_sg = sem("rope_sg")
        s_scl = sem("scl")
        s_setup_in = sem("setup_in")
        s_setup_t = sem("setup_t")
        s_tab_in = sem("tab_in")
        s_tile = sem("tile")
        s_vec_ok = sem("vec_ok")
        s_w_hi = sem("w_hi")
        s_w_lo = sem("w_lo")
        s_x_done = sem("x_done")
        s_x_evac = sem("x_evac")
        s_x_in = sem("x_in")
        s_y_evac = sem("y_evac")
        s_y_t = sem("y_t")
        s_raw_in = [sem(f"raw_in{i}") for i in range(RAW)]
        s_side_read = [sem(f"side_read{i}") for i in range(2)]
        s_att_pe = [sem(f"att_pe{i}") for i in range(2)]
        s_y_out = [sem(f"y_out{i}") for i in range(2)]

        xT = sb("xT", [P, KD, T])
        raw = sb("raw", [P, RAW, CHUNK])
        whi = sb("whi", [P, SPLIT, CHUNK], F32R)
        wlo = sb("wlo", [P, SPLIT, CHUNK], F32R)
        FR1, FR2 = 2 * KD * T, 8 * T
        fra = sb("fra", [P, FR1 + FR2], F32R)
        hF = sb("hF", [P, KD, T])
        BIG = 15026
        big = sb("big", [P, BIG])
        cst = sb("cst_sb", [P, C_N])
        vec = sb("vec", [P, 5 * P])
        mod = sb("mod", [P, LAYERS, 48])
        scl = sb("scl", [P, LAYERS, 2, KD])
        col = sb("col", [P, 24])
        cact = sb("cact", [P, KD])
        wr = sb("wr", [P, LAYERS, KD, 20])
        br = sb("br", [1, LAYERS, 20])
        stat = sb("stat", [P, 64])
        ps = ctx.enter_context(nc.psum_tensor("ps", [P, 8, 512], F32))

        hhi = fra[:, 0:KD * T].rearrange("p (k t) -> p k t", k=KD)
        hlo = fra[:, KD * T:FR1].rearrange("p (k t) -> p k t", k=KD)
        ident = cst[:, C_ID:C_ID + P]
        X1 = [xT[:, k, META:T] for k in range(KD)]
        X2 = [xT[:, k, :] for k in range(KD)]

        def B(off, *shape, n=P):
            size = int(np.prod(shape))
            assert off + size <= BIG, (off, shape)
            v = big[0:n, off:off + size]
            if len(shape) == 2:
                return v.rearrange("p (a b) -> p a b", a=shape[0])
            if len(shape) == 3:
                return v.rearrange("p (a b c) -> p a b c", a=shape[0], b=shape[1])
            return v

        def R2(off, *shape):
            size = int(np.prod(shape))
            assert off + size <= FR2
            return fra[:, FR1 + off:FR1 + off + size].rearrange("p (a b) -> p a b", a=shape[0])

        act_chain = dve_chain = None
        G_Q2, G_K2, G_BF, G_MQ, G_MK, G_B1, G_B2, G_B3, G_FR, G_SUB, G_LAM, G_T = range(12)

        chunks = []

        def chunk(kind, parts, tiles=2):
            chunks.append((kind, parts, tiles))
            return len(chunks) - 1

        def blk(src, k, c0, c1):
            return (0, k, c1 - c0, src[:, c0:c1])

        ada = [[chunk("ada", [blk(cc["w_ada"][l], KD, 256 * j, 256 * j + 256)]) for j in range(24)]
               for l in range(LAYERS)]
        chunks_of_ada = ada[0] + ada[1]
        fox_in, mla_w, moe_w, hy_w = [], [], [[], []], []
        w = cc["fox_w_in"][0]
        for g in range(4):
            fox_in.append([chunk("w", [blk(w, KD, s * D + 256 * g, s * D + 256 * g + 256)], 4 if s == 2 else 2)
                           for s in range(3)])
        fox_out = [chunk("w", [blk(cc["fox_w_out"][0], KD, 256 * j, 256 * j + 256)]) for j in range(4)]

        def moe_chunks(l):
            down = cc["moe_w_down"][l].rearrange("e f d -> (e f) d")
            gate = lambda e: chunk("w", [blk(cc["moe_w_gate"][l, e], KD, 0, E_F)], 2)
            up = lambda e: chunk("w", [blk(cc["moe_w_up"][l, e], KD, 0, E_F)], 2)
            first = gate(0)
            for p in range(E_N // 2):
                ua, gb, ub = up(2 * p), gate(2 * p + 1), up(2 * p + 1)
                ahead = gate(2 * p + 2) if p < E_N // 2 - 1 else None
                rows = down[512 * p:512 * p + 512]
                moe_w[l].append((first, ua, gb, ub, ahead,
                                 [chunk("w", [blk(rows, 4, 512 * j, 512 * j + 512)], 4) for j in range(2)]))
                first = ahead

        moe_chunks(0)
        w = cc["mla_w_in"][0]
        mla_in = [chunk("w", [blk(w, KD, 0, 256)]), chunk("w", [blk(w, KD, 256, 512)]),
                  chunk("w", [blk(w, KD, 512, 672)])]
        for g in range(8):
            mla_w.append(chunk("w", [(0, KQ, 192, cc["mla_w_uq"][0][:, 192 * g:192 * g + 192]),
                                     (KQ * 192, KKV, 256, cc["mla_w_ukv"][0][:, 256 * g:256 * g + 256])], 8))
        mla_out = [chunk("w", [blk(cc["mla_w_out"][0], KD, 256 * j, 256 * j + 256)]) for j in range(4)]
        moe_chunks(1)
        w = cc["hy_w_in_2"][0]
        hy_w = [[None] * 5 for _ in range(HY_G)]
        for g in range(HY_G):
            for c in range(5):
                if c < 4 and hy_w[g][c] is None:
                    c0 = (2, 1, 0, 3)[c] * D_IN + 256 * g
                    hy_w[g][c] = chunk("w", [blk(w, KD, c0, c0 + 256)])
                elif c == 4:
                    if g < HY_G - 1:
                        c0 = 2 * D_IN + 256 * (g + 1)
                        hy_w[g + 1][0] = chunk("w", [blk(w, KD, c0, c0 + 256)])
                    hy_w[g][4] = chunk("w", [blk(cc["hy_w_out_2"][0][256 * g:256 * g + 256], 2, 0, D)], 8)
        DA_UNITS = DA_H * NQ
        DA_STEPS = DA_UNITS + 6
        w = cc["da_w_in_2"][0]
        side, side_at, side_n, side_r = {}, {}, {}, {}

        def da_chunk(kind, g, j=0):
            if kind == "o":
                rows = cc["da_w_out_2"][0][256 * (g - 1):256 * (g + 1)]
                return chunk("w", [blk(rows, 4, 512 * j, 512 * j + 512)], 4)
            c0 = "qkvz".index(kind) * D_IN + 256 * g
            return chunk("w", [blk(w, KD, c0, c0 + 256)], NQ if kind == "v" else 2)

        def opens_chunk(kind, t):
            return t == 0 or kind == "o" and t == 4

        def add_side(where, kind, g, t, b=6, lag=1):
            n = None
            if kind in "qkvzo":
                if opens_chunk(kind, t):
                    side_n[(kind, g)] = da_chunk(kind, g, t // 4)
                n = side_n[(kind, g)]
            f = len(side_at)
            side_at[(kind, g, t)] = f
            if kind == "r":
                side_r[(g, t)] = len(side_r)
            side.setdefault(where, []).append((kind, f, n, g, t, b, lag))

        first = [(k, t) for k in "qk" for t in range(2)] + [("v", t) for t in range(NQ)]
        for i, (k, t) in enumerate(first):
            add_side((-1, 0), k, 0, t, 2 * (i % 4), 4)
        for t in (0, 2):
            add_side((-1, 0), "r", 0, t)
        for h in range(DA_H):
            g, m = divmod(h, 2)
            ahead = g < DA_H // 2 - 1
            if m == 0:
                todo = [("r", g, 1), ("r", g, 3)] + [(k, g + 1, t) for k in "qk" for t in range(2) if ahead]
            else:
                todo = [("z", g, 0)] + [("r", g + 1, t) for t in (0, 2) if ahead] + [("z", g, 1)]
                todo += [("v", g + 1, t) for t in range(NQ) if ahead]
                if g % 2 == 0 and g >= 2:
                    todo += [("o", g - 1, t) for t in range(KD)]
            for i, item in enumerate(todo):
                if h > 0 and i == len(todo) * 7 // 10:
                    add_side((NQ * h + 3, 1), "s", (h - 1) // 2, (h - 1) % 2)
                at = 3 * NQ * i // len(todo)
                if h > 0:
                    at = max(at, 10) if i >= len(todo) * 7 // 10 else min(at, 10)
                add_side((NQ * h + at // 3, at % 3), *item)
        add_side((DA_UNITS + 3, 1), "s", DA_H // 2 - 1, 1)
        for t in range(KD):
            add_side((DA_UNITS + 5, 0), "o", DA_H // 2 - 1, t, (6, 0, 2, 4)[t % 4], 1 if t == 0 else min(t + 1, 4))

        landed, size, split_no, ada_no, tiles_to, total = [], [], {}, {}, [], [0] * RAW
        for n, (kind, parts, tiles) in enumerate(chunks):
            total[n % RAW] += 16 * len(parts)
            landed.append(total[n % RAW])
            size.append(max(o + k * c for o, k, c, _ in parts))
            tiles_to.append((tiles_to[-1] if n else 0) + (tiles if kind == "w" else 0))
            (split_no if kind == "w" else ada_no)[n] = len(split_no if kind == "w" else ada_no)
        order = sorted(split_no)

        def wait_tile(e, n, m):
            before = tiles_to[n] - chunks[n][2]
            e.wait_ge(s_tile, before + m + 1)

        def wait_split(pe, n):
            pe.wait_ge(s_w_lo, split_no[n] + 1)

        def wview(n, k, c, off=0):
            s = split_no[n] % SPLIT
            return [w_[:, s, off:off + k * c].rearrange("p (k c) -> p k c", k=k) for w_ in (whi, wlo)]

        def sp_weights(sp):
            for n, (kind, parts, _) in enumerate(chunks):
                if n in sp_extra:
                    sp_extra[n](sp)
                if n >= RAW:
                    old = n - RAW
                    if old in split_no:
                        sp.wait_ge(s_w_lo, split_no[old] + 1)
                    else:
                        sp.wait_ge(s_ada_used, ada_no[old] + 1)
                for off, k, c, src in parts:
                    dst = raw[:, n % RAW, off:off + k * c].rearrange("p (k c) -> p k c", k=k)
                    sp.dma_start(dst, src.rearrange("(k p) c -> p k c", p=P)).then_inc(s_raw_in[n % RAW], 16)

        def act_split(act, i):
            if i >= len(order):
                return
            n = order[i]
            act.wait_ge(s_raw_in[n % RAW], landed[n])
            if i >= SPLIT:
                act.wait_ge(s_tile, tiles_to[order[i - SPLIT]])
            act.activation(whi[:, i % SPLIT, 0:size[n]], raw[:, n % RAW, 0:size[n]], ACT.Copy).then_inc(s_w_hi, 1)

        def pool_split(pool, i):
            if i >= len(order):
                return
            n = order[i]
            pool.wait_ge(s_w_hi, i + 1)
            pool.tensor_tensor(wlo[:, i % SPLIT, 0:size[n]], raw[:, n % RAW, 0:size[n]],
                               whi[:, i % SPLIT, 0:size[n]], ALU.subtract).then_inc(s_w_lo, 1)

        def mm3(pe, psum, weight, act, start, stop):
            pe.matmul(psum, weight[0], act[0], start=start, stop=False)
            pe.matmul(psum, weight[0], act[1], start=False, stop=False)
            return pe.matmul(psum, weight[1], act[0], start=False, stop=stop)

        class Chain:
            def __init__(self, e, done):
                self.e, self.done, self.n = e, done, 0

            def __call__(self, ins):
                ins.then_inc(self.done, 1)
                self.n += 1
                self.e.wait_ge(self.done, self.n)

            def mark(self, ins):
                ins.then_inc(self.done, 1)
                self.n += 1
                return self.n

            def until(self, n):
                self.e.wait_ge(self.done, n)

        SETUP_IN = 16 * (13 + 12 + 8 + 2)
        VEC_OFF, META_OFF = 4096, 4096 + 5 * P
        x_in = B(0, 4, D)
        meta_in = B(META_OFF, D, n=META)

        def sp_setup(e):
            e.dma_start(cst[:, :], cc["cst"]).then_inc(s_cst_in, 16)
            e.dma_start(x_in, cc["x"][0].rearrange("(i p) d -> p i d", p=P)).then_inc(s_x_in, 16)

        def act_loads(e):
            def rows(tile, r0, src):
                n = src.shape[0]
                e.dma_start(big[r0:r0 + n, VEC_OFF + tile * P:VEC_OFF + tile * P + P], src).then_inc(s_setup_in, 16)

            def split_rows(ap):
                return ap.rearrange("a (k p) -> (a k) p", p=P)

            rows(0, V_C, split_rows(cc["c"]))
            rows(0, V_MIX, split_rows(cc["mix_norm"]))
            rows(0, V_FFN, split_rows(cc["ffn_norm"]))
            rows(0, V_PRE, split_rows(cc["norm_pre_2"]))
            rows(0, V_POST, split_rows(cc["norm_post_2"]))
            rows(0, V_SKIP, split_rows(cc["hy_skip_2"]))
            rows(0, V_QLAT, split_rows(cc["mla_q_lat_norm"]))
            rows(0, V_KVLAT, split_rows(cc["mla_kv_lat_norm"]))
            rows(1, 0, split_rows(cc["b_ada"]))
            rows(2, 0, split_rows(cc["hy_b_in_2"]))
            rows(2, 64, split_rows(cc["hy_conv_b_2"]))
            taps = split_rows(cc["hy_conv_w_2"][0])
            rows(3, 0, taps[0:96])
            rows(4, 0, taps[96:144])

            def column(c, r0, src):
                n = src.shape[1]
                e.dma_start(col[r0:r0 + n, c:c + 1], src.rearrange("o p -> p o")).then_inc(s_setup_in, 16)

            for c, name in ((G_Q2, "fox_q_norm"), (G_K2, "fox_k_norm")):
                column(c, 0, cc[name])
                column(c, 64, cc[name])
            column(G_BF, 0, cc["fox_b_f"])
            column(G_MQ, 0, cc["mla_q_norm"])
            column(G_MK, 0, cc["mla_k_norm"])
            column(G_B1, 0, cc["hy_f_b1_2"])
            column(G_B2, 0, cc["hy_f_b2_2"])
            column(G_B3, 0, cc["hy_f_b3_2"])
            column(G_FR, 0, cc["hy_f_freq_2"])
            column(G_SUB, 0, cc["da_subln_2"])
            for l in range(LAYERS):
                e.dma_start(wr[:, l, :, 0:4], cc["moe_w_grp"][l].rearrange("(k p) c -> p k c", p=P)).then_inc(s_setup_in, 16)
                e.dma_start(wr[:, l, :, 4:20], cc["moe_w_rt"][l].rearrange("(k p) c -> p k c", p=P)).then_inc(s_setup_in, 16)
                e.dma_start(br[:, l, 0:4], cc["moe_b_grp"][l:l + 1]).then_inc(s_setup_in, 16)
                e.dma_start(br[:, l, 4:20], cc["moe_b_rt"][l:l + 1]).then_inc(s_setup_in, 16)
            e.dma_start(meta_in, cc["meta_2"]).then_inc(s_setup_in, 16)
            e.dma_start(f_wf, cc["fox_w_in"][0][:, 3 * D:3 * D + FOX_H].rearrange("(k p) c -> p k c", p=P)).then_inc(s_setup_in, 16)

        def pe_setup(pe):
            pe.wait_ge(s_cst_in, 16)
            pe.wait_ge(s_setup_in, SETUP_IN)
            for t in range(5):
                n = VEC_ROWS[t]
                pe.transpose(ps[:, t // 4, (t % 4) * P:(t % 4) * P + n],
                             big[0:n, VEC_OFF + t * P:VEC_OFF + t * P + P], cst[0:n, C_ID:C_ID + n]).then_inc(s_setup_t, 1)
            pe.wait_ge(s_x_in, 16)
            for k in range(KD):
                if k >= 4:
                    pe.wait_ge(s_x_evac, k - 3)
                for i in range(4):
                    m = pe.transpose(ps[:, 2 + k % 4, P * i:P * i + P], x_in[:, i, P * k:P * k + P], ident)
                m.then_inc(s_setup_t, 1)
            pe.wait_ge(s_setup_in, SETUP_IN)
            for k in range(KD):
                m = pe.transpose(ps[:, 6, META * k:META * k + META], meta_in[:, P * k:P * k + P],
                                 cst[0:META, C_ID:C_ID + META])
            m.then_inc(s_setup_t, 1)

        def dve_setup(e):
            for t in range(5):
                n = VEC_ROWS[t]
                e.wait_ge(s_setup_t, 5)
                e.tensor_copy(vec[:, t * P:t * P + n], ps[:, t // 4, (t % 4) * P:(t % 4) * P + n]).then_inc(s_vec_ok, 1)
            for k in range(KD):
                e.wait_ge(s_setup_t, 5 + k + 1)
                e.tensor_copy(X1[k], ps[:, 2 + k % 4, :]).then_inc(s_x_evac, 1)
            e.wait_ge(s_setup_t, 5 + KD + 1)
            e.tensor_copy(xT[:, :, 0:META], ps[:, 6, 0:KD * META].rearrange("p (k t) -> p k t", k=KD)).then_inc(s_x_evac, 1)

        def act_setup(e):
            e.wait_ge(s_vec_ok, 1)
            e.activation(cact[:, :], vec[:, V_C:V_C + KD], ACT.Silu).then_inc(s_cact, 1)

        NACC = 7

        def ada_to(g):
            return min(1 + 6 * (g + 1), len(chunks_of_ada)) if g >= -1 else 0

        def ada_acc(c):
            o = 4 * T + 192 + 256 * (c % NACC)
            return hF[:, :, :].rearrange("p k t -> p (k t)")[:, o:o + 256]

        def dve_ada_chunks(e, c0, c1):
            for c in range(c0, c1):
                n = chunks_of_ada[c]
                w_ = raw[:, n % RAW, :].rearrange("p (k c) -> p k c", k=KD)
                e.wait_ge(s_cact, 1)
                e.wait_ge(s_raw_in[n % RAW], landed[n])
                if c >= NACC:
                    e.wait_ge(s_ada_pe, c - NACC + 1)
                e.tensor_scalar(ada_acc(c), w_[:, 0, :], cact[:, 0:1], None, ALU.mult).then_inc(s_ada_s, 1)
                for k in range(1, KD):
                    e.wait_ge(s_ada_s, (KD - 1) * c + k)
                    e.scalar_tensor_tensor(out=ada_acc(c), in0=w_[:, k, :], scalar=cact[:, k:k + 1], in1=ada_acc(c),
                                           op0=ALU.mult, op1=ALU.add).then_inc(s_ada_s if k < KD - 1 else s_ada_used, 1)

        def pe_ada_chunks(pe, g):
            for c in range(ada_to(g - 1), ada_to(g)):
                l, j = divmod(c, 24)
                pe.wait_ge(s_ada_used, c + 1)
                for m in range(2):
                    mm = pe.matmul(ps[:, l, 2 * j + m:2 * j + m + 1], ada_acc(c)[:, P * m:P * m + P],
                                   cst[:, C_ONE:C_ONE + 1], start=True, stop=True)
                mm.then_inc(s_ada_pe, 1)

        def pe_ada(pe):
            pe.wait_ge(s_vec_ok, 5)
            pe_filter_group(pe, 0)
            for g in range(HY_G):
                if g < HY_G - 1:
                    pe_filter_group(pe, g + 1)
                pe_filter_l1(pe, g)
                pe_ada_chunks(pe, g - 1)
                pe_filter_dft(pe, g)
            pe_ada_chunks(pe, HY_G - 1)

        def dve_ada(e):
            for l in range(LAYERS):
                e.wait_ge(s_ada_pe, 24 * (l + 1))
                e.wait_ge(s_vec_ok, 5)
                e.tensor_tensor(mod[:, l, :], ps[:, l, 0:48], vec[:, V_BADA + 48 * l:V_BADA + 48 * l + 48],
                                ALU.add).then_inc(s_mod, 1)
                e.wait_ge(s_mod, l + 1)
                for s, (v, c0) in enumerate(((V_MIX, 8), (V_FFN, 32))):
                    e.scalar_tensor_tensor(out=scl[:, l, s, :], in0=mod[:, l, c0:c0 + KD], scalar=1.0,
                                           in1=vec[:, v + KD * l:v + KD * l + KD], op0=ALU.add,
                                           op1=ALU.mult).then_inc(s_scl, 1)

        NORM = [(SEQ, X1)] * 4 + [(T, X2)] * 2
        XD = [0, 8, 72, 80, 144, 152]

        def two(ap_, n):
            return ap_ if n == SEQ else ap_.rearrange("p (a b) -> p a b", a=2)

        def bank(b, n, rows=P):
            return ps[0:rows, b, 0:SEQ] if n == SEQ else ps[0:rows, b:b + 2, 0:HALF]

        def pieces(n):
            return [(0, 0, SEQ)] if n == SEQ else [(0, 0, HALF), (1, HALF, T)]

        def act_norm(e, inst):
            n, src = NORM[inst]
            if inst == 0:
                e.wait_ge(s_hyf_l1, HY_G)
                e.wait_ge(s_ada_pe, len(chunks_of_ada))
                e.wait_ge(s_hyf_st, 16 * HY_G)
                e.wait_ge(s_x_evac, KD + 1)
                e.wait_ge(s_setup_t, 5 + KD + 1)
            if XD[inst] > 0:
                e.wait_ge(s_x_done, XD[inst])
            for k in range(KD):
                e.activation(hF[:, k, 0:n], src[k], ACT.Square).then_inc(s_norm_sq, 1)
            e.wait_ge(s_norm_ss, inst + 1)
            e.activation(two(rs_[:, 0:n], n), bank(0, n), ACT.Sqrt, bias=cst[:, C_EPS:C_EPS + 1]).then_inc(s_norm_rt, 1)
            for k in range(KD):
                e.wait_ge(s_norm_h, KD * inst + k + 1)
                e.activation(hhi[:, k, 0:n], hF[:, k, 0:n], ACT.Copy).then_inc(s_norm_hi, 1)

        def pe_norm(pe, inst):
            n = NORM[inst][0]
            pe.wait_ge(s_mod, 2)
            for k in range(KD):
                pe.wait_ge(s_norm_sq, KD * inst + k + 1)
                for b, t0, t1 in pieces(n):
                    m = pe.matmul(ps[:, b, 0:t1 - t0], cst[:, C_ONED:C_ONED + P], hF[:, k, t0:t1],
                                  start=(k == 0), stop=(k == KD - 1))
            m.then_inc(s_norm_ss, 1)

        def dve_norm(e, inst):
            n, src = NORM[inst]
            rs = rs_[:, 0:n]
            e.wait_ge(s_norm_rt, inst + 1)
            dve_chain(e.reciprocal(rs, rs))
            if inst < 4:
                e.wait_ge(s_scl, 4)
                ok = [dve_chain.mark(e.scalar_tensor_tensor(
                    out=hF[:, k, 0:n], in0=src[k], scalar=scl[:, inst // 2, inst % 2, k:k + 1], in1=rs,
                    op0=ALU.mult, op1=ALU.mult)) for k in range(KD)]
                for k in range(KD):
                    dve_chain.until(ok[k])
                    c0 = 24 * (inst % 2) + k
                    e.tensor_scalar(hF[:, k, 0:n], hF[:, k, 0:n], mod[:, inst // 2, c0:c0 + 1], None,
                                    ALU.add).then_inc(s_norm_h, 1)
            else:
                g0 = V_PRE + KD * (inst - 4)
                for k in range(KD):
                    e.scalar_tensor_tensor(out=hF[:, k, 0:n], in0=src[k], scalar=vec[:, g0 + k:g0 + k + 1],
                                           in1=rs, op0=ALU.mult, op1=ALU.mult).then_inc(s_norm_h, 1)

        def pool_norm(e, inst):
            n = NORM[inst][0]
            for k in range(KD):
                e.wait_ge(s_norm_hi, KD * inst + k + 1)
                e.tensor_tensor(hlo[:, k, 0:n], hF[:, k, 0:n], hhi[:, k, 0:n], ALU.subtract).then_inc(s_norm_lo, 1)

        def hsp(k, t0, t1):
            return [hhi[:, k, t0:t1], hlo[:, k, t0:t1]]

        def pe_proj(pe, inst, n, m, b0, ntok, c0=None):
            w_ = wview(n, KD, size[n] // KD)
            c0 = P * m if c0 is None else c0
            for b, t0, t1 in pieces(ntok):
                for k in range(KD):
                    if b == 0 and m == 0:
                        pe.wait_ge(s_norm_lo, KD * inst + k + 1)
                    mm = mm3(pe, ps[:, b0 + b, 0:t1 - t0], [v[:, k, c0:c0 + P] for v in w_], hsp(k, t0, t1),
                             k == 0, k == KD - 1)
            mm.then_inc(s_tile, 1)

        AP_, AT, AD = 0, 3 * SEQ, 5 * SEQ
        a_p = [B(AP_ + SEQ * i, SEQ) for i in range(3)]
        a_pt = [B(AT + SEQ * i, SEQ) for i in range(2)]
        a_dg = [B(AD + P * i, P) for i in range(3)]
        A_END = AD + 3 * P
        UNITS = 64
        ATT_STEPS = UNITS + 3
        PT_BANK, O_BANK, SIDE_BANK = 3, 5, 6
        aside, aside_at = [{}, {}], [{}, {}]
        side_count = [0]

        def add_aside(l, where, kind, g, q):
            f = None
            if kind != "n":
                f = side_count[0]
                side_count[0] += 1
                aside_at[l][(kind, g, q)] = f
            aside[l].setdefault(where, []).append((kind, f, g, q))

        todo = [[], []]
        for g in range(4):
            at = 32 * (g - 1)
            for q in range(4):
                todo[0] += [(at + 2 * q, "p", g, q), (at + 8 + 3 * q, "v", g, q), (at + 9 + 3 * q, "s", g, q),
                            (at + 13 + 4 * q, "n", g, q)]
                h = 4 * g + q
                todo[0].append((8 * h - 4, "g", g, q))
        for g in range(8):
            at = 16 * (g - 1)
            todo[1].append((at + 4, "v", g, 0))
            for q, (p_, s_, n_, r_) in enumerate(((0, 3, 6, 10), (2, 6, 9, 13), (6, 10, 13, 17), (8, 12, 16, 20))):
                todo[1] += [(at + p_, "p", g, q), (at + s_, "s", g, q), (at + n_, "n", g, q), (at + r_, "r", g, q)]
        for l in range(2):
            for at, k, g, q in sorted(todo[l], key=lambda x: (x[0], x[2])):
                add_aside(l, (at // 2, at % 2) if at >= 0 else (-1, 0), k, g, q)

        def side_bank(f):
            return SIDE_BANK + f % 2

        def wait_side(e, l, kind, g, q):
            f = aside_at[l][(kind, g, q)]
            e.wait_ge(s_side_read[f % 2], f // 2 + 1)

        def unit(u):
            return u // 4, u % 4

        def pe_attn(pe, l, side_of, q_of, k_of, v_of, ready, v_ready):
            side_of(pe, -1, 0)
            for s in range(ATT_STEPS):
                U = UNITS * l + s
                if s < UNITS:
                    h, i = unit(s)
                    ready(h, i)
                    nk = P * (i + 1)
                    if U >= 3:
                        pe.wait_ge(s_att_ex, U - 2)
                        pe.wait_ge(s_att_mx, U - 2)
                    pe.matmul(ps[:, U % 3, 0:nk], q_of(h, i), k_of(h, nk), start=True, stop=False)
                    pe.matmul(ps[:, U % 3, nk - P:nk], ident, cst[:, C_MASK:C_MASK + P], start=False,
                              stop=True).then_inc(s_att_s, 1)
                side_of(pe, s, 0)
                u, U = s - 3, UNITS * l + s - 3
                if 0 <= u < UNITS:
                    h, i = unit(u)
                    b = 64 * (h % 2)
                    v_ready(h, i)
                    if U >= 8 and u % 8 == 0:
                        pe.wait_ge(s_att_of, U // 8)
                    pe.wait_ge(s_att_pe[U % 2], U // 2 + 1)
                    for kt in range(i + 1):
                        m = pe.matmul(ps[b:b + 64, O_BANK, P * i:P * i + P], v_of(h, kt),
                                      a_pt[U % 2][:, P * kt:P * kt + P], start=(kt == 0), stop=(kt == i))
                    m.then_inc(s_att_pv, 1)
                side_of(pe, s, 1)
                u, U = s - 2, UNITS * l + s - 2
                if 0 <= u < UNITS:
                    h, i = unit(u)
                    pe.wait_ge(s_att_dg, U + 1)
                    if U >= 2:
                        pe.wait_ge(s_att_pe[U % 2], U // 2)
                    for kt in range(i + 1):
                        m = pe.matmul(ps[:, PT_BANK + U % 2, P * kt:P * kt + P], a_p[U % 3][:, P * kt:P * kt + P],
                                      a_dg[U % 3], start=True, stop=True)
                    m.then_inc(s_att_pt, 1)

        def act_attn(e, l, side_of, scale, src):
            side_of(e, -1, 0)
            for s in range(ATT_STEPS):
                U = UNITS * l + s
                if s < UNITS:
                    n = P * (s % 4 + 1)
                    e.wait_ge(s_att_mx, U + 1)
                    if U >= 3:
                        e.wait_ge(s_att_pt, U - 2)
                        e.wait_ge(s_att_ri, U - 2)
                    e.activation(a_p[U % 3][:, 0:n], src(U, n), ACT.Exp, scale=scale, bias=stat[:, U % 3:U % 3 + 1],
                                 accum_out=stat[:, 4 + U % 3:5 + U % 3]).then_inc(s_att_ex, 1)
                side_of(e, s, 0)
                side_of(e, s, 1)
                if 0 <= s - 2 < UNITS and s % 2 == 0:
                    copy_pt(e, UNITS * l + s - 2, e.copy)

        def dve_attn(e, l, side_of, maximum):
            side_of(e, -1, 0)
            for s in range(ATT_STEPS + 1):
                if s < UNITS:
                    maximum(s, UNITS * l + s)
                if 0 <= s - 1 < UNITS:
                    U = UNITS * l + s - 1
                    e.wait_ge(s_att_ex, U + 1)
                    e.reciprocal(stat[:, 8 + U % 3:9 + U % 3], stat[:, 4 + U % 3:5 + U % 3]).then_inc(s_att_ri, 1)
                    e.wait_ge(s_att_ri, U + 1)
                    if U >= 3:
                        e.wait_ge(s_att_pt, U - 2)
                    e.tensor_scalar(a_dg[U % 3], ident, stat[:, 8 + U % 3:9 + U % 3], None,
                                    ALU.mult).then_inc(s_att_dg, 1)
                side_of(e, s, 0)
                if (s - 4) % 8 == 7 and s - 4 > 0:
                    pair = (UNITS * l + s - 4) // 8
                    e.wait_ge(s_att_pv, 8 * pair + 8)
                    e.tensor_copy(hF[:, pair % 8, 0:SEQ], ps[:, O_BANK, :]).then_inc(s_att_of, 1)
                side_of(e, s, 1)
                if 0 <= s - 2 < UNITS and s % 2:
                    copy_pt(e, UNITS * l + s - 2, e.tensor_copy)

        def copy_pt(e, U, copy):
            n = P * (U % 4 + 1)
            e.wait_ge(s_att_pt, U + 1)
            if U >= 2:
                e.wait_ge(s_att_pv, U - 1)
            copy(a_pt[U % 2][:, 0:n], ps[:, PT_BANK + U % 2, 0:n]).then_inc(s_att_pe[U % 2], 1)

        FO = A_END
        f_qk = [B(FO + 2048 * i, 4, SEQ) for i in range(2)]
        f_sq = B(FO + 4096, 4, SEQ)
        f_nb = B(FO + 6144, 2, SEQ)
        f_cu = B(FO + 7168, 5, SEQ, n=FOX_H)
        f_v = [B(FO + 9728, 4, 256), B(FO + 7168, 4, 256)]
        f_wf = B(BIG - P, KD, FOX_H)
        rs_ = B(BIG - P - T, T)
        assert FO + 10752 <= BIG - P - T

        def pe_fox_side(pe, s, slot):
            for kind, f, g, q in aside[0].get((s, slot), ()):
                if kind == "n":
                    continue
                b = side_bank(f)
                if f >= 2:
                    pe.wait_ge(s_side_read[f % 2], f // 2)
                if kind == "p":
                    n = fox_in[g][q // 2]
                    wait_split(pe, n)
                    pe_proj(pe, 0, n, q % 2, b, SEQ)
                elif kind == "v":
                    n = fox_in[g][2]
                    wait_split(pe, n)
                    w_ = wview(n, KD, 256)
                    for k in range(KD):
                        mm = mm3(pe, ps[:, b, 0:256], hsp(k, P * q, P * q + P), [x[:, k, :] for x in w_],
                                 k == 0, k == KD - 1)
                    mm.then_inc(s_tile, 1)
                elif kind == "s":
                    pe.wait_ge(s_fox_sq, 4 * g + q + 1)
                    pe.matmul(ps[:, b, :], cst[:, C_B64:C_B64 + P], f_sq[:, q, :], start=True,
                              stop=True).then_inc(s_fox_ss, 1)
                else:
                    h = 4 * g + q
                    pe.wait_ge(s_fox_cum, 1)
                    pe.matmul(ps[:, b, :], cst[0:FOX_H, C_ID + h:C_ID + h + 1].to_broadcast([FOX_H, P]), f_cu[:, 2, :],
                              start=True, stop=True).then_inc(s_fox_nb, 1)

        def pe_fox(pe):
            pe.wait_ge(s_setup_in, SETUP_IN)
            for k in range(KD):
                pe.wait_ge(s_norm_h, k + 1)
                m = pe.matmul(ps[0:FOX_H, 7, :], f_wf[:, k, :], hF[:, k, 0:SEQ], start=(k == 0), stop=(k == KD - 1))
            m.then_inc(s_fox_f, 1)
            pe.wait_ge(s_norm_rt, 1)
            pe.wait_ge(s_fox_fz, 1)

            def ready(h, i):
                if h % 4 == 0 and i == 0:
                    pe.wait_ge(s_fox_qk, h + 4)

            def v_ready(h, i):
                if h % 4 == 0 and i == 0:
                    for q in (2, 3):
                        wait_side(pe, 0, "v", h // 4, q)

            pe_attn(pe, 0, pe_fox_side,
                    lambda h, i: f_qk[h // 4 % 2][64 * (h % 2):64 * (h % 2) + 64, h % 4 // 2, P * i:P * i + P],
                    lambda h, nk: f_qk[h // 4 % 2][64 * (h % 2):64 * (h % 2) + 64, 2 + h % 4 // 2, 0:nk],
                    lambda h, kt: f_v[h // 4 % 2][:, kt, 64 * (h % 4):64 * (h % 4) + 64], ready, v_ready)

        def act_fox_side(e, s, slot):
            for kind, f, g, q in aside[0].get((s, slot), ()):
                if kind == "p":
                    if q % 2 == 0:
                        act_split(e, split_no[fox_in[g][q // 2]] + 1)
                    wait_side(e, 0, "p", g, q)
                    if g > 0:
                        e.wait_ge(s_fox_qk, 4 * g)
                    e.activation(f_sq[:, q, :], f_qk[g % 2][:, q, :], ACT.Square).then_inc(s_fox_sq, 1)
                elif kind == "v":
                    n = fox_in[g][2]
                    if q == 0:
                        act_split(e, split_no[n] + 1)
                    wait_tile(e, n, q)
                    if g == 1:
                        e.wait_ge(s_fox_cum, 1)
                    elif g >= 2:
                        e.wait_ge(s_att_pv, 16 * (g - 1))
                    e.activation(f_v[g % 2][:, q, :], ps[:, side_bank(f), 0:256], ACT.Copy).then_inc(s_side_read[f % 2], 1)
                elif kind == "s":
                    e.wait_ge(s_fox_ss, 4 * g + q + 1)
                    e.activation(f_sq[:, q, :], ps[:, side_bank(f), :], ACT.Sqrt,
                                 bias=cst[:, C_EPS:C_EPS + 1]).then_inc(s_side_read[f % 2], 1)
                elif kind == "g":
                    h = 4 * g + q
                    e.wait_ge(s_fox_nb, h + 1)
                    if h >= 2:
                        e.wait_ge(s_att_mx, 4 * (h - 1))
                    e.activation(f_nb[:, h % 2, :], ps[:, side_bank(f), :], ACT.Copy).then_inc(s_side_read[f % 2], 1)

        def act_fox(e):
            e.wait_ge(s_fox_f, 1)
            e.wait_ge(s_setup_in, SETUP_IN)
            e.activation(f_cu[:, 0, :], ps[0:FOX_H, 7, :], ACT.Identity, bias=col[0:FOX_H, G_BF:G_BF + 1]).then_inc(s_fox_fz, 1)
            e.wait_ge(s_fox_fz, 1)
            act_chain(e.activation(f_cu[:, 1, :], f_cu[:, 0, :], ACT.Abs))
            act_chain(e.activation(f_cu[:, 3, :], f_cu[:, 1, :], ACT.Exp, scale=-1.0))
            e.activation(f_cu[:, 4, :], f_cu[:, 3, :], ACT.Ln, bias=cst[0:FOX_H, C_ONE:C_ONE + 1]).then_inc(s_fox_ln, 1)
            act_attn(e, 0, act_fox_side, -1.0, lambda U, n: a_p[U % 3][:, 0:n])

        def dve_fox_side(e, s, slot):
            for kind, f, g, q in aside[0].get((s, slot), ()):
                if kind == "p":
                    wait_tile(e, fox_in[g][q // 2], q % 2)
                    if g >= 2:
                        e.wait_ge(s_att_s, 16 * (g - 1))
                    e.tensor_copy(f_qk[g % 2][:, q, :], ps[:, side_bank(f), :]).then_inc(s_side_read[f % 2], 1)
                elif kind == "n":
                    wait_side(e, 0, "s", g, q)
                    dve_chain(e.reciprocal(f_sq[:, q, :], f_sq[:, q, :]))
                    gc = G_Q2 if q < 2 else G_K2
                    v = f_qk[g % 2][:, q, :]
                    e.scalar_tensor_tensor(out=v, in0=v, scalar=col[:, gc:gc + 1],
                                           in1=f_sq[:, q, :], op0=ALU.mult, op1=ALU.mult).then_inc(s_fox_qk, 1)

        def dve_fox(e):
            e.wait_ge(s_fox_ln, 1)
            dve_chain(e.scalar_tensor_tensor(out=f_cu[:, 1, :], in0=f_cu[:, 0, :], scalar=0.0, in1=f_cu[:, 4, :],
                                             op0=ALU.min, op1=ALU.subtract))
            dve_chain(e.memset(f_cu[:, 3, :], 1.0))
            dve_chain(e.tensor_tensor_scan(f_cu[:, 0, :], f_cu[:, 3, :], f_cu[:, 1, :], 0.0, ALU.mult, ALU.add))
            e.tensor_scalar(f_cu[:, 2, :], f_cu[:, 0, :], -float(FOX_D) ** 0.5, None, ALU.mult).then_inc(s_fox_cum, 1)

            def maximum(s, U):
                h, i = unit(s)
                wait_side(e, 0, "g", h // 4, h % 4)
                e.wait_ge(s_att_s, U + 1)
                if U >= 3:
                    e.wait_ge(s_att_pt, U - 2)
                n = P * i + P
                e.tensor_tensor_reduce(a_p[U % 3][:, 0:n], ps[:, U % 3, 0:n], f_nb[:, h % 2, 0:n],
                                       -float(FOX_D) ** -0.5, 3e38, ALU.add, ALU.min,
                                       stat[:, U % 3:U % 3 + 1]).then_inc(s_att_mx, 1)

            dve_attn(e, 0, dve_fox_side, maximum)

        def pool_fox(e):
            for g in range(4):
                for n in fox_in[g]:
                    pool_split(e, split_no[n] + 1)

        def act_out(e, l, outs):
            for k in range(KD):
                e.wait_ge(s_att_of, KD * l + k + 1)
                e.activation(hhi[:, k, 0:SEQ], hF[:, k, 0:SEQ], ACT.Copy).then_inc(s_o_hi, 1)
            for n in outs:
                act_split(e, split_no[n] + 1)

        def pool_out(e, l, outs):
            for k in range(KD):
                e.wait_ge(s_o_hi, KD * l + k + 1)
                e.tensor_tensor(hlo[:, k, 0:SEQ], hF[:, k, 0:SEQ], hhi[:, k, 0:SEQ], ALU.subtract).then_inc(s_o_lo, 1)
            for n in outs:
                pool_split(e, split_no[n] + 1)

        def pe_out(pe, l, outs):
            for j, n in enumerate(outs):
                wait_split(pe, n)
                w_ = wview(n, KD, 256)
                for m in range(2):
                    t = 2 * j + m
                    if t >= 4:
                        pe.wait_ge(s_x_done, XD[2 * l] + t - 3)
                    for k in range(KD):
                        pe.wait_ge(s_o_lo, KD * l + k + 1)
                        mm = mm3(pe, ps[:, t % 4, :], [v[:, k, P * m:P * m + P] for v in w_], hsp(k, 0, SEQ),
                                 k == 0, k == KD - 1)
                    mm.then_inc(s_tile, 1)

        def dve_out(e, l, outs):
            for t in range(KD):
                wait_tile(e, outs[t // 2], t % 2)
                e.scalar_tensor_tensor(out=X1[t], in0=ps[:, t % 4, :], scalar=mod[:, l, 16 + t:17 + t], in1=X1[t],
                                       op0=ALU.mult, op1=ALU.add).then_inc(s_x_done, 1)

        m_cb = B(0, E_N, SEQ)
        m_sg = B(8192, 4, SEQ)
        m_t = B(10240, 4, SEQ)
        m_ct = B(12288, SEQ, n=E_N)
        m_lt = B(12288, SEQ, n=20)
        MS = 12800
        m_lg = B(MS, 4, 20)
        m_a, m_b = B(MS + 80, 4, 16), B(MS + 144, 4, 16)
        m_f = [B(MS + 208 + 16 * i, 4, 4) for i in range(12)]
        hid = fra[:, FR1:FR1 + 8 * SEQ].rearrange("p (s k t) -> p s k t", s=2, k=4)

        def pe_moe(pe, l):
            inst = 2 * l + 1
            pe.wait_ge(s_setup_in, SETUP_IN)
            for k in range(KD):
                pe.wait_ge(s_norm_h, KD * inst + k + 1)
                m = pe.matmul(ps[0:20, 6, :], wr[:, l, k, :], hF[:, k, 0:SEQ], start=(k == 0), stop=(k == KD - 1))
            m.then_inc(s_moe_lt, 1)

            def into(x, n, up):
                wait_split(pe, n)
                for m in range(2):
                    if x > 0 and up:
                        pe.wait_ge(s_moe_u, 2 * (x - 1) + m + 1)
                    elif x > 0:
                        pe.wait_ge(s_moe_sg, 2 * (x - 1) + m + 1)
                    pe_proj(pe, inst, n, m, 2 * up + m, SEQ)

            pe.wait_ge(s_norm_rt, inst + 1)
            pe.wait_ge(s_moe_ls, l + 1)
            for i in range(4):
                o = ps[:, 7, 32 * i:32 * i + 20]
                pe.matmul(o, m_lt[:, P * i:P * i + P], cst[0:20, C_ID:C_ID + 20], start=True, stop=False)
                m = pe.matmul(o, cst[0:1, C_ONE:C_ONE + P], br[:, l, :], start=False, stop=True)
            m.then_inc(s_moe_lg, 1)
            into(E_N * l, moe_w[l][0][0], 0)
            pe.wait_ge(s_moe_cb, l + 1)
            for i in range(4):
                m = pe.transpose(ps[0:E_N, 6, P * i:P * i + P], m_b[:, i, :], ident)
            m.then_inc(s_moe_ct, 1)
            pe.wait_ge(s_moe_cts, l + 1)
            for r in range(E_N):
                if E_N * l + r - 1 > 0:
                    pe.wait_ge(s_moe_bc, E_N * l + r - 1)
                pe.matmul(ps[:, 4 + r % 2, :], cst[0:E_N, C_ID + r:C_ID + r + 1].to_broadcast([E_N, P]), m_ct,
                          start=True, stop=True).then_inc(s_moe_b, 1)
            for p in range(8):
                _, ua, gb, ub, ahead, downs = moe_w[l][p]
                x = E_N * l + 2 * p
                into(x, ua, 1)
                into(x + 1, gb, 0)
                into(x + 1, ub, 1)
                if ahead is not None:
                    into(x + 2, ahead, 0)
                for j, n in enumerate(downs):
                    wait_split(pe, n)
                    w_ = wview(n, 4, 512)
                    for m in range(4):
                        t = 4 * j + m
                        if p == 0 and j == 0:
                            pe.wait_ge(s_moe_bc, E_N * l + E_N)
                        else:
                            pe.wait_ge(s_x_done, XD[inst] + 8 * p + t - 3)
                        for k in range(4):
                            pe.wait_ge(s_moe_hl, 4 * (8 * l + p) + k + 1)
                            mm = mm3(pe, ps[:, 4 + m, :], [v[:, k, P * m:P * m + P] for v in w_],
                                     [hid[:, s, k, :] for s in range(2)], k == 0, k == 3)
                        mm.then_inc(s_tile, 1)

        def act_moe(e, l):
            e.wait_ge(s_moe_lt, l + 1)
            e.activation(m_lt, ps[0:20, 6, :], ACT.Copy).then_inc(s_moe_ls, 1)
            for i in range(2):
                e.wait_ge(s_moe_re, 2 * l + i + 1)
                v = m_f[0] if i == 0 else m_f[8][:, :, 0:1]
                e.activation(v, v, ACT.Exp).then_inc(s_moe_rx, 1)

            def silu(x, n):
                for m in range(2):
                    wait_tile(e, n, m)
                    if 2 * (x - 2) + m + 1 > 0:
                        e.wait_ge(s_moe_u, 2 * (x - 2) + m + 1)
                    e.activation(m_sg[:, 2 * (x % 2) + m, :], ps[:, m, :], ACT.Silu).then_inc(s_moe_sg, 1)

            def split_hidden(x):
                for m in range(2):
                    e.wait_ge(s_moe_t, 2 * x + m + 1)
                    e.activation(hid[:, 0, 2 * (x % 2) + m, :], m_t[:, 2 * (x % 2) + m, :], ACT.Copy).then_inc(s_moe_hh, 1)

            first = moe_w[l][0][0]
            act_split(e, split_no[first] + 1)
            silu(E_N * l, first)
            e.wait_ge(s_moe_ct, l + 1)
            e.activation(m_ct, ps[0:E_N, 6, :], ACT.Copy).then_inc(s_moe_cts, 1)
            for r in range(E_N):
                e.wait_ge(s_moe_b, E_N * l + r + 1)
                e.activation(m_cb[:, r, :], ps[:, 4 + r % 2, :], ACT.Copy).then_inc(s_moe_bc, 1)
            for p in range(8):
                _, ua, gb, ub, ahead, downs = moe_w[l][p]
                x = E_N * l + 2 * p
                act_split(e, split_no[ua] + 1)
                split_hidden(x)
                act_split(e, split_no[gb] + 1)
                silu(x + 1, gb)
                act_split(e, split_no[ub] + 1)
                split_hidden(x + 1)
                if ahead is not None:
                    act_split(e, split_no[ahead] + 1)
                    silu(x + 2, ahead)
                for n in downs:
                    act_split(e, split_no[n] + 1)

        def pool_moe(e, l):
            first = moe_w[l][0][0]
            pool_split(e, split_no[first] + 1)

            def split_hidden(x):
                for m in range(2):
                    t = 2 * (x % 2) + m
                    e.wait_ge(s_moe_hh, 2 * x + m + 1)
                    e.tensor_tensor(hid[:, 1, t, :], m_t[:, t, :], hid[:, 0, t, :], ALU.subtract).then_inc(s_moe_hl, 1)

            for p in range(8):
                _, ua, gb, ub, ahead, downs = moe_w[l][p]
                x = E_N * l + 2 * p
                pool_split(e, split_no[ua] + 1)
                split_hidden(x)
                pool_split(e, split_no[gb] + 1)
                pool_split(e, split_no[ub] + 1)
                split_hidden(x + 1)
                for n in ([ahead] if ahead is not None else []) + downs:
                    pool_split(e, split_no[n] + 1)

        def dve_moe(e, l):
            c = dve_chain
            bc = lambda v: v.to_broadcast([P, 4, 4])
            e.wait_ge(s_moe_lg, l + 1)
            c(e.tensor_copy(m_lg, ps[:, 7, 0:128].rearrange("p (i c) -> p i c", i=4)[:, :, 0:20]))

            def pick(out, eq, scratch):
                ne, run = scratch
                c(e.tensor_scalar(ne, eq, -1.0, 1.0, ALU.mult, ALU.add))
                c(e.tensor_copy(out, eq))
                c(e.tensor_copy(run, ne))
                for j in range(1, 4):
                    c(e.tensor_tensor(out[:, :, j:j + 1], eq[:, :, j:j + 1], run[:, :, j - 1:j], ALU.mult))
                    c(e.tensor_tensor(run[:, :, j:j + 1], ne[:, :, j:j + 1], run[:, :, j - 1:j], ALU.mult))

            gl = m_lg[:, :, 0:4]
            mx = m_f[1][:, :, 0:1]
            c(e.tensor_reduce(mx, gl, AX_X, ALU.max))
            e.tensor_tensor(m_f[0], gl, bc(mx), ALU.subtract).then_inc(s_moe_re, 1)
            c(e.tensor_tensor(m_f[2], gl, bc(mx), ALU.is_equal))
            pick(m_f[3], m_f[2], (m_f[4], m_f[5]))
            e.wait_ge(s_moe_rx, 2 * l + 1)
            c(e.tensor_reduce(m_f[1][:, :, 1:2], m_f[0], AX_X, ALU.add))
            c(e.reciprocal(m_f[1][:, :, 2:3], m_f[1][:, :, 1:2]))
            el = m_lg[:, :, 4:20].rearrange("p i (g j) -> p i g j", g=4)
            gm = m_f[3].unsqueeze(3).to_broadcast([P, 4, 4, 4])
            c(e.tensor_tensor(m_a.rearrange("p i (g j) -> p i g j", g=4), el, gm, ALU.mult))
            c(e.tensor_reduce(m_f[2], m_a.rearrange("p i (g j) -> p i j g", g=4), AX_X, ALU.add))
            c(e.tensor_reduce(m_f[1][:, :, 3:4], m_f[2], AX_X, ALU.max))
            c(e.tensor_tensor(m_f[4], m_f[2], bc(m_f[1][:, :, 3:4]), ALU.is_equal))
            pick(m_f[5], m_f[4], (m_f[6], m_f[7]))
            c(e.scalar_tensor_tensor(out=m_f[2], in0=m_f[5], scalar=NEG, in1=m_f[2], op0=ALU.mult, op1=ALU.add))
            c(e.tensor_reduce(m_f[8][:, :, 1:2], m_f[2], AX_X, ALU.max))
            c(e.tensor_tensor(m_f[4], m_f[2], bc(m_f[8][:, :, 1:2]), ALU.is_equal))
            pick(m_f[9], m_f[4], (m_f[6], m_f[7]))
            e.tensor_tensor(m_f[8][:, :, 0:1], m_f[8][:, :, 1:2], m_f[1][:, :, 3:4], ALU.subtract).then_inc(s_moe_re, 1)
            e.wait_ge(s_moe_rx, 2 * l + 2)
            w1, w2 = m_f[10][:, :, 0:1], m_f[10][:, :, 1:2]
            c(e.tensor_scalar(w2, m_f[8][:, :, 0:1], 1.0, None, ALU.add))
            c(e.reciprocal(w1, w2))
            c(e.tensor_tensor(w1, w1, m_f[1][:, :, 2:3], ALU.mult))
            c(e.tensor_tensor(w2, w1, m_f[8][:, :, 0:1], ALU.mult))
            c(e.tensor_tensor(m_f[5], m_f[5], bc(w1), ALU.mult))
            c(e.tensor_tensor(m_f[9], m_f[9], bc(w2), ALU.mult))
            c(e.tensor_tensor(m_f[5], m_f[5], m_f[9], ALU.add))
            ew = m_f[5].unsqueeze(2).to_broadcast([P, 4, 4, 4])
            e.tensor_tensor(m_b.rearrange("p i (g j) -> p i g j", g=4), ew, gm, ALU.mult).then_inc(s_moe_cb, 1)

            def hidden(x, n):
                for m in range(2):
                    t = 2 * (x % 2) + m
                    wait_tile(e, n, m)
                    e.wait_ge(s_moe_sg, 2 * x + m + 1)
                    if 2 * (x - 2) + m + 1 > 0:
                        e.wait_ge(s_moe_hl, 2 * (x - 2) + m + 1)
                    e.tensor_tensor(m_t[:, t, :], m_sg[:, t, :], ps[:, 2 + m, :], ALU.mult).then_inc(s_moe_u, 1)
                for m in range(2):
                    t = 2 * (x % 2) + m
                    e.wait_ge(s_moe_u, 2 * x + m + 1)
                    e.wait_ge(s_moe_bc, x + 1)
                    e.tensor_tensor(m_t[:, t, :], m_t[:, t, :], m_cb[:, x % E_N, :], ALU.mult).then_inc(s_moe_t, 1)

            for p in range(8):
                _, ua, gb, ub, ahead, downs = moe_w[l][p]
                x = E_N * l + 2 * p
                hidden(x, ua)
                hidden(x + 1, ub)
                for t in range(KD):
                    wait_tile(e, downs[t // 4], t % 4)
                    e.wait_ge(s_x_done, XD[2 * l + 1] + 8 * p + t - 7)
                    e.scalar_tensor_tensor(out=X1[t], in0=ps[:, 4 + t % 4, :], scalar=mod[:, l, 40 + t:41 + t],
                                           in1=X1[t], op0=ALU.mult, op1=ALU.add).then_inc(s_x_done, 1)

        MO = A_END
        l_c, l_s = B(MO, SEQ, n=MLA_QK), B(MO + SEQ, SEQ, n=MLA_QK)
        MT = (0, 2, 1, 3)
        l_raw, l_sq = (B(MO + 1024 + 2048 * i, 4, SEQ, n=MLA_QK) for i in range(2))
        l_kn = B(MO + 5120, 2, SEQ, n=MLA_QK)
        l_qf = [B(MO + 6144 + 2048 * i, 4, SEQ, n=MLA_QK) for i in range(2)]
        l_v = [B(MO + 10240 + 512 * i, 4, P) for i in range(2)]
        assert MO + 11264 <= BIG - P - T
        l_sq5 = B(MO + 1024, KQ + KKV, SEQ)
        l_kr = B(MO + 1024 + 3072, 2, SEQ)
        l_rs = B(MO + 6144, 2, SEQ)
        lat = hF[:, 0:KQ + KKV, 0:SEQ]
        lat_sp = [v.rearrange("p k t -> p (k t)")[:, 0:5 * SEQ].rearrange("p (k t) -> p k t", k=5) for v in (hhi, hlo)]

        def l_qn(t):
            return l_raw[:, t, :] if t < 2 else l_kn[:, t - 2, :]

        def reduce_angle(e, a_, k_):
            c = dve_chain
            c(e.tensor_scalar(k_, a_, 1.0 / (2 * float(np.pi)), ROUND, ALU.mult, ALU.add))
            c(e.tensor_scalar(k_, k_, ROUND, None, ALU.subtract))
            for part in (TWO_PI_1, TWO_PI_2, TWO_PI_3):
                c(e.scalar_tensor_tensor(out=a_, in0=k_, scalar=-part, in1=a_, op0=ALU.mult, op1=ALU.add))
            c(e.tensor_scalar(a_, a_, PI_IN, -PI_IN, ALU.min, ALU.max))

        def pe_mla_side(pe, s, slot):
            for kind, f, g, q in aside[1].get((s, slot), ()):
                if kind == "n":
                    continue
                b = side_bank(f)
                if f >= 2:
                    pe.wait_ge(s_side_read[f % 2], f // 2)
                n = mla_w[g]
                wait_split(pe, n)
                if kind == "p":
                    a_ = MT[q] % 2
                    k0, nk, rows, c0, w_ = ((0, KQ, MLA_QK, 96 * a_, wview(n, KQ, 192)) if q % 2 == 0 else
                                            (KQ, KKV, P, P * a_, wview(n, KKV, 256, KQ * 192)))
                    for k in range(nk):
                        pe.wait_ge(s_lat_lo, k0 + k + 1)
                        mm = mm3(pe, ps[0:rows, b, :], [v[:, k, c0:c0 + rows] for v in w_],
                                 [v[:, k0 + k, :] for v in lat_sp], k == 0, k == nk - 1)
                    mm.then_inc(s_tile, 1)
                elif kind == "v":
                    w_ = wview(n, KKV, 256, KQ * 192)
                    for i in range(4):
                        for k in range(KKV):
                            mm = mm3(pe, ps[:, b, P * i:P * i + P], [v[:, KQ + k, P * i:P * i + P] for v in lat_sp],
                                     [v[:, k, :].rearrange("p (h c) -> p h c", h=2)[:, :, 64:128] for v in w_],
                                     k == 0, k == KKV - 1)
                        mm.then_inc(s_tile, 1)
                elif kind == "s":
                    pe.wait_ge(s_mla_sq, 4 * g + q + 1)
                    pe.matmul(ps[0:MLA_QK, b, :], cst[0:MLA_QK, C_O96:C_O96 + MLA_QK], l_sq[:, MT[q], :],
                              start=True, stop=True).then_inc(s_mla_ss, 1)
                else:
                    pe.wait_ge(s_mla_qn, 4 * g + q + 1)
                    pe.matmul(ps[0:MLA_QK, b, :], cst[0:MLA_QK, C_R96:C_R96 + MLA_QK], l_qn(MT[q]),
                              start=True, stop=True).then_inc(s_mla_rq, 1)

        def pe_mla(pe):
            pe.wait_ge(s_norm_rt, 3)
            for j, n in enumerate(mla_in):
                wait_split(pe, n)
                for m in range(2):
                    pe_proj(pe, 2, n, m, 2 * j + m, SEQ, c0=None if j < 2 else 32 * m)
            for r, (k0, k1, ones) in enumerate(((0, KQ, C_O384), (KQ, KQ + KKV, C_O256))):
                for k in range(k0, k1):
                    pe.wait_ge(s_lat_sq, k + 1)
                    m = pe.matmul(ps[:, 6 + r, :], cst[:, ones:ones + P], l_sq5[:, k, :], start=(k == k0), stop=(k == k1 - 1))
                m.then_inc(s_lat_ss, 1)
            pe.wait_ge(s_lat_kr, 2)
            pe.wait_ge(s_lat_cp, 5)
            pe.wait_ge(s_lat_rt, 2)

            def ready(h, i):
                if i == 0:
                    pe.wait_ge(s_mla_qf, 2 * (h + 1))

            def v_ready(h, i):
                if h % 2 == 0 and i == 0:
                    wait_side(pe, 1, "v", h // 2, 0)

            pe_attn(pe, 1, pe_mla_side, lambda h, i: l_qf[h // 2 % 2][:, h % 2, P * i:P * i + P],
                    lambda h, nk: l_qf[h // 2 % 2][:, 2 + h % 2, 0:nk],
                    lambda h, kt: l_v[h // 2 % 2][:, kt, 64 * (h % 2):64 * (h % 2) + 64], ready, v_ready)

        def act_mla_side(e, s, slot):
            for kind, f, g, q in aside[1].get((s, slot), ()):
                if kind == "p":
                    if q == 0:
                        act_split(e, split_no[mla_w[g]] + 1)
                    wait_side(e, 1, "p", g, q)
                    e.wait_ge(s_lat_kr, 2)
                    if g > 0:
                        e.wait_ge(s_mla_qf, 4 * (g - 1) + q + 1)
                    e.activation(l_sq[:, MT[q], :], l_raw[:, MT[q], :], ACT.Square).then_inc(s_mla_sq, 1)
                elif kind == "v":
                    wait_tile(e, mla_w[g], 5)
                    if g >= 2:
                        e.wait_ge(s_att_pv, UNITS + 8 * (g - 1))
                    e.activation(l_v[g % 2], ps[:, side_bank(f), :].rearrange("p (i c) -> p i c", i=4),
                                 ACT.Copy).then_inc(s_side_read[f % 2], 1)
                elif kind == "s":
                    e.wait_ge(s_mla_ss, 4 * g + q + 1)
                    e.activation(l_sq[:, MT[q], :], ps[0:MLA_QK, side_bank(f), :], ACT.Sqrt,
                                 bias=cst[0:MLA_QK, C_EPS:C_EPS + 1]).then_inc(s_side_read[f % 2], 1)

        def act_mla(e):
            e.wait_ge(s_rope_r, 1)
            e.activation(l_s, l_kr[0:MLA_QK, 0, :], ACT.Sin).then_inc(s_rope_s, 1)
            act_chain(e.activation(l_kr[0:MLA_QK, 1, :], l_kr[0:MLA_QK, 0, :], ACT.Abs))
            e.activation(l_c, l_kr[0:MLA_QK, 1, :], ACT.Sin, scale=-1.0, bias=cst[0:MLA_QK, C_HPI:C_HPI + 1]).then_inc(s_rope_s, 1)
            for j, n in enumerate(mla_in):
                act_split(e, split_no[n] + 1)
                for m in range(2):
                    t = 2 * j + m
                    if t < 5:
                        wait_tile(e, n, m)
                        e.activation(l_sq5[:, t, :], ps[:, t, :], ACT.Square).then_inc(s_lat_sq, 1)
            for r in range(2):
                e.wait_ge(s_lat_ss, r + 1)
                e.activation(l_rs[:, r, :], ps[:, 6 + r, :], ACT.Sqrt, bias=cst[:, C_EPS:C_EPS + 1]).then_inc(s_lat_rt, 1)
            wait_tile(e, mla_in[2], 1)
            e.wait_ge(s_lat_ss, 2)
            for a_ in range(2):
                e.activation(l_raw[MLA_NOPE:MLA_QK, 2 + a_, :], ps[96:P, 5, :], ACT.Copy).then_inc(s_lat_kr, 1)
            for k in range(5):
                e.wait_ge(s_lat_n, k + 1)
                e.activation(lat_sp[0][:, k, :], lat[:, k, :], ACT.Copy).then_inc(s_lat_hi, 1)
            act_attn(e, 1, act_mla_side, 1.0, lambda U, n: ps[:, U % 3, 0:n])

        def pool_mla(e):
            for n in mla_in:
                pool_split(e, split_no[n] + 1)
            for k in range(5):
                e.wait_ge(s_lat_hi, k + 1)
                e.tensor_tensor(lat_sp[1][:, k, :], lat[:, k, :], lat_sp[0][:, k, :], ALU.subtract).then_inc(s_lat_lo, 1)
            for g in range(8):
                pool_split(e, split_no[mla_w[g]] + 1)
                e.wait_ge(s_rope_s, 2)
                for q in range(4):
                    e.wait_ge(s_mla_qn, 4 * g + q + 1)
                    e.tensor_tensor(l_sq[:, MT[q], :], l_qn(MT[q]), l_c, ALU.mult).then_inc(s_mla_t1, 1)
                    wait_side(e, 1, "r", g, q)
                    e.wait_ge(s_mla_t1, 4 * g + q + 1)
                    v = l_qf[g % 2][:, MT[q], :]
                    e.tensor_tensor(v, v, l_sq[:, MT[q], :], ALU.add).then_inc(s_mla_qf, 1)

        def sp_mla(e):
            e.wait_ge(s_x_done, XD[2])
            e.dma_start(l_kr[0:MLA_QK, 1, :].bitcast(I32), cc["positions"].partition_broadcast(MLA_QK)).then_inc(s_pos_in, 16)

        def dve_mla_side(e, s, slot):
            for kind, f, g, q in aside[1].get((s, slot), ()):
                if kind == "p":
                    wait_tile(e, mla_w[g], q if q < 2 else q + 4)
                    e.wait_ge(s_lat_ss, 2)
                    if g > 0:
                        e.wait_ge(s_mla_sq, 4 * (g - 1) + q + 1)
                        e.wait_ge(s_mla_t1, 4 * (g - 1) + q + 1)
                        e.wait_ge(s_mla_rq, 4 * (g - 1) + q + 1)
                    rows = MLA_QK if q % 2 == 0 else MLA_NOPE
                    e.tensor_copy(l_raw[0:rows, MT[q], :], ps[0:rows, side_bank(f), :]).then_inc(s_side_read[f % 2], 1)
                elif kind == "n":
                    gc = G_T if MT[q] < 2 else G_MK
                    wait_side(e, 1, "s", g, q)
                    dve_chain(e.reciprocal(l_sq[:, MT[q], :], l_sq[:, MT[q], :]))
                    e.wait_ge(s_lat_kr, 2)
                    if g > 0:
                        e.wait_ge(s_mla_t1, 4 * (g - 1) + q + 1)
                        e.wait_ge(s_mla_rq, 4 * (g - 1) + q + 1)
                    e.scalar_tensor_tensor(out=l_qn(MT[q]), in0=l_raw[:, MT[q], :], scalar=col[0:MLA_QK, gc:gc + 1],
                                           in1=l_sq[:, MT[q], :], op0=ALU.mult, op1=ALU.mult).then_inc(s_mla_qn, 1)
                elif kind == "r":
                    e.wait_ge(s_mla_rq, 4 * g + q + 1)
                    e.wait_ge(s_rope_sg, 1)
                    if g >= 2:
                        e.wait_ge(s_att_s, UNITS + 8 * (g - 1))
                    e.tensor_tensor(l_qf[g % 2][:, MT[q], :], ps[0:MLA_QK, side_bank(f), :], l_s,
                                    ALU.mult).then_inc(s_side_read[f % 2], 1)

        def dve_mla(e):
            c = dve_chain
            e.wait_ge(s_pos_in, 16)
            e.wait_ge(s_setup_in, SETUP_IN)
            a_, k_ = l_kr[0:MLA_QK, 0, :], l_kr[0:MLA_QK, 1, :]
            c(e.tensor_copy(a_, k_.bitcast(I32)))
            c(e.tensor_scalar(a_, a_, cst[0:MLA_QK, C_INVF:C_INVF + 1], None, ALU.mult))
            reduce_angle(e, a_, k_)
            e.tensor_scalar(col[0:MLA_QK, G_T:G_T + 1], col[0:MLA_QK, G_MQ:G_MQ + 1], float(MLA_QK) ** -0.5, None,
                            ALU.mult).then_inc(s_rope_r, 1)
            e.wait_ge(s_rope_s, 1)
            e.tensor_scalar(l_s, l_s, cst[0:MLA_QK, C_SGN:C_SGN + 1], None, ALU.mult).then_inc(s_rope_sg, 1)
            for t in range(5):
                wait_tile(e, mla_in[t // 2], t % 2)
                e.wait_ge(s_lat_sq, t + 1)
                e.tensor_copy(lat[:, t, :], ps[:, t, :]).then_inc(s_lat_cp, 1)
            ok = []
            for r in range(2):
                e.wait_ge(s_lat_rt, r + 1)
                ok.append(dve_chain.mark(e.reciprocal(l_rs[:, r, :], l_rs[:, r, :])))
            for t in range(5):
                r = int(t >= KQ)
                v = V_QLAT + t if t < KQ else V_KVLAT + t - KQ
                dve_chain.until(ok[r])
                e.wait_ge(s_lat_cp, t + 1)
                e.scalar_tensor_tensor(out=lat[:, t, :], in0=lat[:, t, :], scalar=vec[:, v:v + 1], in1=l_rs[:, r, :],
                                       op0=ALU.mult, op1=ALU.mult).then_inc(s_lat_n, 1)

            def maximum(s, U):
                e.wait_ge(s_att_s, U + 1)
                e.wait_ge(s_att_ex, U - 2)
                e.tensor_reduce(stat[:, U % 3:U % 3 + 1], ps[:, U % 3, 0:P * (U % 4 + 1)], AX_X, ALU.max,
                                negate=True).then_inc(s_att_mx, 1)

            dve_attn(e, 1, dve_mla_side, maximum)

        spec = nc.dram_tensor("spec", (HY_G, TQ, NQ * 512), F32, kind="Internal").ap()
        h_tab = B(0, 2, NQ, NQ * TQ)[0:TQ]
        f_S, f_C = B(0, NQ, 512)[0:TQ], B(2560, NQ, 512)[0:TQ]
        f_F, f_B = B(5300, NQ, 512)[0:TQ], B(7860, NQ, 512)[0:TQ]
        f_rd = B(12212, 2, 256)[0:TQ]
        TAB = 2 * NQ * NQ * TQ
        f_tab = [fra[0:TQ, TAB * i:TAB * i + TAB].rearrange("p (s a b) -> p s a b", s=2, a=NQ) for i in range(2)]

        def f_sp(g, i):
            if g % 2 == 0:
                return [v.rearrange("p s c -> p (s c)")[0:QS[i], 512 * i:512 * i + 512] for v in (whi[:, :, :], wlo[:, :, :])]
            rest = [fra[:, 2 * TAB + 512 * q:2 * TAB + 512 * q + 512] for q in range(4)]
            for v in (whi, wlo):
                rest += [v[:, :, :].rearrange("p s c -> p (s c)")[:, 2560 + 512 * q:3072 + 512 * q] for q in range(3)]
            return [rest[q][0:QS[i], :] for q in (i, NQ + i)]

        F_TILES = (1, 2, 3, 4, 0)
        f_dec = B(10420, NQ, 256)[0:TQ]
        f_w4 = B(11700, 2, 256)[0:HY_HID]
        hflat = hF[:, :, :].rearrange("p k t -> p (k t)")
        f_feat = hflat[0:HY_EMB, 0:T]
        f_ang, f_mul, f_hid = (hflat[0:HY_HID, T * i:T * i + T] for i in (1, 2, 3))
        f_w = [hflat[0:(HY_EMB, HY_HID, HY_HID)[i], 4 * T + 64 * i:4 * T + 64 * i + 64] for i in range(3)]
        l1n = sb("l1n", [P, 16])

        def act_filter_loads(e):
            e.dma_start(f_feat, cc["feats"]).then_inc(s_hyf_in, 16)
            for i in range(3):
                e.dma_start(f_w[i], cc[f"hy_f_w{i + 1}_2"][0]).then_inc(s_hyf_in, 16)
            e.wait_ge(s_x_evac, KD + 1)
            e.wait_ge(s_vec_ok, 5)
            e.dma_start(h_tab.rearrange("p a b c -> p (a b c)"), cc["dft"]).then_inc(s_tab_in, 16)
            filter_group_loads(e, 0)

        def filter_group_loads(e, g):
            if g > 0:
                e.wait_ge(s_hyf_F, NQ * g)
            c0 = 256 * g
            for i in range(NQ):
                e.dma_start(f_dec[0:QS[i], i, :], cc["decay"][TQ * i:TQ * i + QS[i], c0:c0 + 256]).then_inc(s_hyf_d, 16)
            e.dma_start(f_w4, cc["hy_f_w4_2"][0].rearrange("k (d c) -> k d c", d=2)[:, :, c0:c0 + 256]).then_inc(s_hyf_d, 16)

        def pe_filter_mlp(pe):
            pe.wait_ge(s_hyf_in, 64)
            pe.wait_ge(s_x_evac, KD)
            for i in range(3):
                if i > 0:
                    pe.wait_ge(s_hyf_sin, i)
                for h in range(2):
                    m = pe.matmul(ps[0:HY_HID, 2 + h, 0:HALF], f_w[i],
                                  (f_feat if i == 0 else f_hid)[:, HALF * h:HALF * h + HALF], start=True, stop=True)
                m.then_inc(s_hyf_l, 1)

        def dve_filter_mlp(e):
            e.wait_ge(s_setup_in, SETUP_IN)
            for i in range(3):
                e.wait_ge(s_hyf_l, i + 1)
                if i > 0:
                    e.wait_ge(s_hyf_sin, i)
                dve_chain(e.tensor_scalar(two(f_ang, T), bank(2, T, HY_HID), col[0:HY_HID, G_B1 + i:G_B1 + i + 1],
                                          col[0:HY_HID, G_FR:G_FR + 1], ALU.add, ALU.mult))
                reduce_angle(e, f_ang, f_mul)
                e.memset(stat[0:1, 63:64], 0.0).then_inc(s_hyf_a, 1)

        def act_filter_mlp(e):
            for i in range(3):
                e.wait_ge(s_hyf_a, i + 1)
                e.activation(f_hid, f_ang, ACT.Sin).then_inc(s_hyf_sin, 1)

        def pe_filter_group(pe, g):
            pe.wait_ge(s_hyf_d, 96 * (g + 1))
            pe.wait_ge(s_hyf_sin, 3)
            for i in range(NQ):
                n = NQ * g + i
                r = QS[i]
                if n - 1 > 0:
                    pe.wait_ge(s_hyf_F, n - 1)
                for d in range(2):
                    m = pe.matmul(ps[0:r, 4 + n % 2, 256 * d:256 * d + 256], f_hid[:, TQ * i:TQ * i + r], f_w4[:, d, :],
                                  start=True, stop=True)
                m.then_inc(s_hyf_f, 1)

        def pe_filter_l1(pe, g):
            pe.wait_ge(s_hyf_rd, 2 * g + 2)
            for ct in range(2):
                for q in range(2):
                    rows = (TQ, QS[NQ - 1])[q]
                    m = pe.matmul(ps[:, 2, 2 * g + ct:2 * g + ct + 1], f_rd[0:rows, q, P * ct:P * ct + P],
                                  cst[0:rows, C_ONE:C_ONE + 1], start=(q == 0), stop=(q == 1))
            m.then_inc(s_hyf_l1, 1)

        def pe_filter_dft(pe, g):
            pe.wait_ge(s_hyf_tb, 2)
            for j in range(NQ):
                n = NQ * g + j
                if n - 1 > 0:
                    pe.wait_ge(s_hyf_e, n - 1)
                for s in range(2):
                    for q, i in enumerate(F_TILES):
                        pe.wait_ge(s_hyf_lo, NQ * g + q + 1)
                        m = mm3(pe, ps[0:TQ, 6 + n % 2, 256 * s:256 * s + 256],
                                [v[0:QS[i], s, i, TQ * j:TQ * j + TQ] for v in f_tab],
                                [v[:, 256 * s:256 * s + 256] for v in f_sp(g, i)], q == 0, q == NQ - 1)
                m.then_inc(s_hyf_H, 1)

        def dve_filter_table(e):
            e.wait_ge(s_hyf_tb, 1)
            e.tensor_tensor(f_tab[1], h_tab, f_tab[0], ALU.subtract).then_inc(s_hyf_tb, 1)

        def act_filter_table(e):
            e.wait_ge(s_tab_in, 16)
            e.activation(f_tab[0], h_tab, ACT.Copy).then_inc(s_hyf_tb, 1)

        def dve_filter_group(e, g):
            for i in range(NQ):
                n, r = NQ * g + i, QS[i]
                e.wait_ge(s_hyf_f, n + 1)
                if g > 0:
                    e.wait_ge(s_hyf_h, 2 * NQ * g)
                e.tensor_tensor(f_F[0:r, i, :].rearrange("p (d c) -> p d c", d=2),
                                ps[0:r, 4 + n % 2, :].rearrange("p (d c) -> p d c", d=2),
                                f_dec[0:r, i, :].unsqueeze(1).to_broadcast([r, 2, 256]), ALU.mult).then_inc(s_hyf_F, 1)
            e.wait_ge(s_hyf_A, NQ * g + 1)
            e.tensor_scalar(f_F[:, 0, 256:512], f_F[:, 0, 256:512], cst[0:TQ, C_M0:C_M0 + 1], None,
                            ALU.mult).then_inc(s_hyf_m, 1)
            e.wait_ge(s_hyf_A, NQ * g + NQ)
            if g > 0:
                e.wait_ge(s_hyf_l1, g)
            for q in range(2):
                i0, i1, rows = ((0, NQ - 1, TQ), (NQ - 1, NQ, QS[NQ - 1]))[q]
                e.tensor_reduce(f_rd[0:rows, q, :], f_B[0:rows, i0:i1, :].rearrange("p i (d c) -> p c i d", d=2),
                                AX_XY, ALU.add).then_inc(s_hyf_rd, 1)

        def act_filter_abs(e, g):
            for i in range(NQ):
                e.wait_ge(s_hyf_F, NQ * g + i + 1)
                if g > 0:
                    e.wait_ge(s_hyf_rd, 2 * g)
                e.activation(f_B[0:QS[i], i, :], f_F[0:QS[i], i, :], ACT.Abs).then_inc(s_hyf_A, 1)
            for q, i in enumerate(F_TILES):
                e.wait_ge(s_hyf_h, 2 * (NQ * g + q) + 2)
                if g >= 2:
                    e.wait_ge(s_hyf_H, NQ * (g - 1))
                e.activation(f_sp(g, i)[0], f_C[0:QS[i], i, :], ACT.Copy).then_inc(s_hyf_hi, 1)

        def pool_filter_group(e, g):
            e.wait_ge(s_hyf_tb, 2)
            for i in F_TILES:
                e.wait_ge(s_hyf_F, NQ * g + i + 1)
                if i == 0:
                    e.wait_ge(s_hyf_m, g + 1)
                if g > 0:
                    e.wait_ge(s_hyf_lo, NQ * g)
                f, b = f_F[0:QS[i], i, 0:256], f_F[0:QS[i], i, 256:512]
                e.tensor_tensor(f_C[0:QS[i], i, 0:256], f, b, ALU.add).then_inc(s_hyf_h, 1)
                e.tensor_tensor(f_C[0:QS[i], i, 256:512], f, b, ALU.subtract).then_inc(s_hyf_h, 1)
            for q, i in enumerate(F_TILES):
                hi, lo = f_sp(g, i)
                e.wait_ge(s_hyf_hi, NQ * g + q + 1)
                e.tensor_tensor(lo, f_C[0:QS[i], i, :], hi, ALU.subtract).then_inc(s_hyf_lo, 1)

        def act_filter_store(e, g):
            if g > 0:
                e.wait_ge(s_hyf_st, 16 * g)
            e.wait_ge(s_hyf_tb, 2)
            for j in range(NQ):
                n = NQ * g + j
                e.wait_ge(s_hyf_H, n + 1)
                e.activation(f_S[:, j, :], ps[0:TQ, 6 + n % 2, :], ACT.Copy,
                             scale=cst[0:TQ, C_WF + j:C_WF + j + 1]).then_inc(s_hyf_e, 1)
            e.wait_ge(s_hyf_e, NQ * (g + 1))
            e.dma_start(spec[g], f_S.rearrange("p a b -> p (a b)")).then_inc(s_hyf_st, 16)

        def dve_filter_norm(e):
            e.wait_ge(s_hyf_l1, HY_G)
            dve_chain(e.tensor_scalar(l1n[:, :], ps[:, 2, 0:16], EPS, None, ALU.add))
            dve_chain(e.reciprocal(l1n[:, :], l1n[:, :]))

        h_P = B(5300, NQ, 512)[0:TQ]
        h_W, h_G = B(7860, 2, T), B(8916, 2, T)
        h_T = B(9972, 2, T)
        h_t = B(9972, 2, 512)[0:TQ]
        h_u = B(11028, 2, T + 2)
        h_wt = B(12088, NQ, 256)[0:TQ]
        yg = fra[:, FR1:FR1 + 4 * T].rearrange("p (s k t) -> p s k t", s=2, k=2)
        STREAM = (2, 1, 0)

        def pe_hyena(pe):
            pe.wait_ge(s_norm_rt, 5)

            def first_product(g):
                wait_split(pe, hy_w[g][0])
                if g > 0:
                    pe.wait_ge(s_hy_te, NQ * g)
                    pe.wait_ge(s_hy_m, NQ * g)
                for m in range(2):
                    pe_proj(pe, 4, hy_w[g][0], m, 2 * m, T)

            first_product(0)
            for g in range(HY_G):
                ch = hy_w[g]
                for c in range(1, 4):
                    wait_split(pe, ch[c])
                    for m in range(2):
                        if c == 1:
                            if 2 * g > 0:
                                pe.wait_ge(s_hy_c, 2 * g)
                        else:
                            if c == 2 and g > 0:
                                pe.wait_ge(s_hy_a, 8 * g)
                            pe.wait_ge(s_hy_u, 6 * g + 2 * (c - 2) + m + 1)
                        pe_proj(pe, 4, ch[c], m, 4 * (c % 2) + 2 * m, T)
                for i in range(NQ):
                    r, n = QS[i], NQ * g + i
                    if n - 1 > 0:
                        pe.wait_ge(s_hy_te, n - 1)
                    pe.wait_ge(s_hy_u, 6 * g + 6)
                    for m in range(2):
                        pe.wait_ge(s_hy_w, 2 * g + m + 1)
                        mm = pe.transpose(ps[0:r, n % 2, P * m:P * m + P], h_W[:, m, TQ * i:TQ * i + r], ident)
                    mm.then_inc(s_hy_t, 1)
                if g == 0:
                    pe.wait_ge(s_tab_in, 32)
                for j in range(NQ):
                    n = NQ * g + j
                    if n - 1 > 0:
                        pe.wait_ge(s_hy_m, n - 1)
                    for s in range(2):
                        for i in range(NQ):
                            pe.wait_ge(s_hy_te, NQ * g + i + 1)
                            mm = pe.matmul(ps[0:TQ, 2 + n % 2, 256 * s:256 * s + 256],
                                           h_tab[0:QS[i], s, i, TQ * j:TQ * j + TQ], h_wt[0:QS[i], i, :],
                                           start=(i == 0), stop=(i == NQ - 1))
                    mm.then_inc(s_hy_v, 1)
                for m in range(2):
                    pe.wait_ge(s_hy_z, 2 * g + 2)
                    for h in range(2):
                        for s in range(2):
                            for j in range(NQ):
                                pe.wait_ge(s_hy_p, 2 * (NQ * g + j) + s + 1)
                                mm = pe.matmul(ps[:, 4 + 2 * m + h, 0:HALF], h_P[:, j, 256 * s + P * m:256 * s + P * m + P],
                                               h_tab[:, s, j, HALF * h:HALF * h + HALF], start=(s + j == 0),
                                               stop=(s + j == NQ))
                    mm.then_inc(s_hy_i, 1)
                if g < HY_G - 1:
                    first_product(g + 1)
                n = ch[4]
                wait_split(pe, n)
                w_ = wview(n, 2, D)
                for t in range(KD):
                    if 8 * g + t - 1 > 0:
                        pe.wait_ge(s_hy_a, 8 * g + t - 1)
                    if t < 2:
                        pe.wait_ge(s_hy_te, NQ * (g + 1))
                        pe.wait_ge(s_hy_m, NQ * (g + 1))
                        if g < HY_G - 1:
                            pe.wait_ge(s_hy_u, 6 * g + 8)
                    for b, t0, t1 in pieces(T):
                        for k in range(2):
                            pe.wait_ge(s_hy_yl, 2 * g + k + 1)
                            mm = mm3(pe, ps[:, 2 * (t % 2) + b, 0:HALF], [v[:, k, P * t:P * t + P] for v in w_],
                                     [yg[:, s, k, t0:t1] for s in range(2)], k == 0, k == 1)
                    mm.then_inc(s_tile, 1)

        def act_hyena(e):
            e.dma_start(h_tab.rearrange("p a b c -> p (a b c)"), cc["dft"]).then_inc(s_tab_in, 16)

            def copy_product(g, c):
                n = hy_w[g][c]
                for m in range(2):
                    wait_tile(e, n, m)
                    if c:
                        e.wait_ge(s_hy_cv, 6 * g + 2 * (c - 1) + m + 1)
                    else:
                        if g > 0:
                            e.wait_ge(s_hy_g, 2 * (g - 1) + m + 1)
                        e.wait_ge(s_hy_pad, 1)
                    v = V_HYB + 16 * STREAM[c] + 2 * g + m
                    e.activation(two(h_u[:, m, 1:T + 1], T), bank(4 * (c % 2) + 2 * m, T), ACT.Identity,
                                 bias=vec[:, v:v + 1]).then_inc(s_hy_u, 1)
                if c == 0:
                    if g > 0:
                        e.wait_ge(s_hy_i, 2 * g)
                    e.dma_start(h_P.rearrange("p a b -> p (a b)"), spec[g]).then_inc(s_hy_H, 16)

            act_split(e, split_no[hy_w[0][0]] + 1)
            copy_product(0, 0)
            for g in range(HY_G):
                ch = hy_w[g]
                for c in (1, 2):
                    act_split(e, split_no[ch[c]] + 1)
                    copy_product(g, c)
                act_split(e, split_no[ch[3]] + 1)
                for m in range(2):
                    wait_tile(e, ch[3], m)
                    e.wait_ge(s_hy_cv, 6 * g + 4 + m + 1)
                    v = V_HYB + 48 + 2 * g + m
                    e.activation(two(h_u[:, m, 1:T + 1], T), bank(4 + 2 * m, T), ACT.Silu,
                                 bias=vec[:, v:v + 1]).then_inc(s_hy_z, 1)
                for i in range(NQ):
                    e.wait_ge(s_hy_t, NQ * g + i + 1)
                    if g > 0:
                        e.wait_ge(s_hy_v, NQ * g)
                    e.activation(h_wt[0:QS[i], i, :], ps[0:QS[i], (NQ * g + i) % 2, 0:256], ACT.Copy).then_inc(s_hy_te, 1)
                if g < HY_G - 1:
                    act_split(e, split_no[hy_w[g + 1][0]] + 1)
                for m in range(2):
                    e.wait_ge(s_hy_yg, 2 * g + m + 1)
                    if g > 0:
                        e.wait_ge(s_tile, tiles_to[hy_w[g - 1][4]])
                    e.activation(yg[:, 0, m, :], h_W[:, m, :], ACT.Copy).then_inc(s_hy_yh, 1)
                if g < HY_G - 1:
                    copy_product(g + 1, 0)
                act_split(e, split_no[ch[4]] + 1)

        def pool_hyena(e):
            pool_split(e, split_no[hy_w[0][0]] + 1)
            for g in range(HY_G):
                ch = hy_w[g]
                for c in range(1, 4):
                    pool_split(e, split_no[ch[c]] + 1)
                for j in range(NQ):
                    e.wait_ge(s_hy_m, NQ * g + j + 1)
                    e.tensor_tensor(h_P[:, j, 0:256], h_t[:, 0, 0:256], h_t[:, 0, 256:512], ALU.subtract).then_inc(s_hy_p, 1)
                    e.tensor_tensor(h_P[:, j, 256:512], h_t[:, 1, 0:256], h_t[:, 1, 256:512], ALU.add).then_inc(s_hy_p, 1)
                if g < HY_G - 1:
                    pool_split(e, split_no[hy_w[g + 1][0]] + 1)
                for m in range(2):
                    e.wait_ge(s_hy_yh, 2 * g + m + 1)
                    e.tensor_tensor(yg[:, 1, m, :], h_W[:, m, :], yg[:, 0, m, :], ALU.subtract).then_inc(s_hy_yl, 1)
                pool_split(e, split_no[ch[4]] + 1)

        def dve_hyena(e):
            c_ = dve_chain
            for m in range(2):
                e.memset(h_u[:, m, 0:1], 0.0)
                ins = e.memset(h_u[:, m, T + 1:T + 2], 0.0)
            c_(ins)
            e.memset(stat[0:1, 62:63], 0.0).then_inc(s_hy_pad, 1)
            e.wait_ge(s_hy_pad, 1)
            for g in range(HY_G):
                for c in range(3):
                    dst = (h_W, h_T, h_G)[c]
                    for m in range(2):
                        i = 16 * STREAM[c] + 2 * g + m
                        u, d = h_u[:, m, :], dst[:, m, :]
                        e.wait_ge(s_hy_u, 6 * g + 2 * c + m + 1)
                        if c == 0:
                            if 2 * g > 0:
                                e.wait_ge(s_hy_yl, 2 * g)
                        if c == 1:
                            if 2 * NQ * g > 0:
                                e.wait_ge(s_hy_p, 2 * NQ * g)
                        c_(e.tensor_scalar(d, u[:, 0:T], vec[:, V_CW + i:V_CW + i + 1], vec[:, V_CB + i:V_CB + i + 1],
                                           ALU.mult, ALU.add))
                        c_(e.scalar_tensor_tensor(out=d, in0=u[:, 1:T + 1], scalar=vec[:, V_CW + 48 + i:V_CW + 49 + i],
                                                  in1=d, op0=ALU.mult, op1=ALU.add))
                        e.scalar_tensor_tensor(out=d, in0=u[:, 2:T + 2], scalar=vec[:, V_CW2 + i:V_CW2 + i + 1], in1=d,
                                               op0=ALU.mult, op1=ALU.add).then_inc(s_hy_cv, 1)
                    if c == 1:
                        for m in range(2):
                            e.wait_ge(s_hy_cv, 6 * g + 2 + m + 1)
                            e.tensor_tensor(h_W[:, m, :], h_W[:, m, :], h_T[:, m, :], ALU.mult).then_inc(s_hy_w, 1)
                for m in range(2):
                    e.wait_ge(s_hy_z, 2 * g + m + 1)
                    e.wait_ge(s_hy_cv, 6 * g + 4 + m + 1)
                    e.tensor_tensor(h_G[:, m, :], h_G[:, m, :], h_u[:, m, 1:T + 1], ALU.mult).then_inc(s_hy_g, 1)
                e.wait_ge(s_hy_H, 16 * (g + 1))
                e.wait_ge(s_hy_w, 2 * g + 2)
                for j in range(NQ):
                    n = NQ * g + j
                    b = 2 + n % 2
                    e.wait_ge(s_hy_v, n + 1)
                    if 2 * n > 0:
                        e.wait_ge(s_hy_p, 2 * n)
                    e.tensor_tensor(h_t[:, 0, :], h_P[:, j, :], ps[0:TQ, b, :], ALU.mult)
                    e.tensor_tensor(h_t[:, 1, 0:256], h_P[:, j, 0:256], ps[0:TQ, b, 256:512], ALU.mult)
                    e.tensor_tensor(h_t[:, 1, 256:512], h_P[:, j, 256:512], ps[0:TQ, b, 0:256], ALU.mult).then_inc(s_hy_m, 1)
                ok = []
                for m in range(2):
                    i = 2 * g + m
                    e.wait_ge(s_hy_t, NQ * (g + 1))
                    ok.append(c_.mark(e.tensor_scalar(h_W[:, m, :], h_W[:, m, :], vec[:, V_SKIP + i:V_SKIP + i + 1],
                                                      None, ALU.mult)))
                for m in range(2):
                    i = 2 * g + m
                    e.wait_ge(s_hy_i, i + 1)
                    c_.until(ok[m])
                    w2 = two(h_W[:, m, :], T)
                    e.scalar_tensor_tensor(out=w2, in0=bank(4 + 2 * m, T), scalar=l1n[:, i:i + 1], in1=w2,
                                           op0=ALU.mult, op1=ALU.add).then_inc(s_hy_c, 1)
                for m in range(2):
                    e.wait_ge(s_hy_c, 2 * g + m + 1)
                    e.wait_ge(s_hy_g, 2 * g + m + 1)
                    e.tensor_tensor(h_W[:, m, :], h_W[:, m, :], h_G[:, m, :], ALU.mult).then_inc(s_hy_yg, 1)
                add_output(e, hy_w[g][4], g == 0, s_hy_a, 8 * g, range(KD), lambda t: 2 * (t % 2))

        def add_output(e, n, first, added, at, ts, b_of):
            for q, t in enumerate(ts):
                wait_tile(e, n, q)
                y2 = two(hF[:, t, :], T)
                if first:
                    e.tensor_copy(y2, bank(b_of(t), T)).then_inc(added, 1)
                else:
                    e.wait_ge(added, at + q - KD + 1)
                    e.tensor_tensor(y2, y2, bank(b_of(t), T), ALU.add).then_inc(added, 1)

        y_sq = B(0, KD, T)
        POST_AT = ((s_hy_a, 8 * HY_G), (s_da_fe, len(side_at)))

        def act_post(e, q):
            for k in range(KD):
                e.wait_ge(POST_AT[q][0], POST_AT[q][1])
                e.activation(y_sq[:, k, :], hF[:, k, :], ACT.Square).then_inc(s_post_sq, 1)
            e.wait_ge(s_post_ss, q + 1)
            e.activation(two(rs_, T), bank(0, T), ACT.Sqrt, bias=cst[:, C_EPS:C_EPS + 1]).then_inc(s_post_rt, 1)

        def pe_post(pe, q):
            pe.wait_ge(POST_AT[q][0], POST_AT[q][1])
            for k in range(KD):
                pe.wait_ge(s_post_sq, KD * q + k + 1)
                for b, t0, t1 in pieces(T):
                    m = pe.matmul(ps[:, b, 0:HALF], cst[:, C_ONED:C_ONED + P], y_sq[:, k, t0:t1],
                                  start=(k == 0), stop=(k == KD - 1))
            m.then_inc(s_post_ss, 1)

        def dve_post(e, q):
            e.wait_ge(s_post_rt, q + 1)
            dve_chain(e.reciprocal(rs_, rs_))
            e.wait_ge(POST_AT[q][0], POST_AT[q][1])
            ok = [dve_chain.mark(e.scalar_tensor_tensor(
                out=hF[:, k, :], in0=hF[:, k, :], scalar=vec[:, V_POST + KD * q + k:V_POST + KD * q + k + 1], in1=rs_,
                op0=ALU.mult, op1=ALU.mult)) for k in range(KD)]
            for k in range(KD):
                dve_chain.until(ok[k])
                e.tensor_tensor(X2[k], X2[k], hF[:, k, :], ALU.add).then_inc(s_x_done, 1)

        d_tab = B(0, 2, T)
        d_raw, d_qf = B(1056, 4, T), B(3168, 4, T)
        d_z, d_o = B(5280, 2, T), B(6336, 2, T)
        d_v = [B(7392 + 1280 * i, NQ, 256)[0:TQ] for i in range(2)]
        d_p = B(9952, 3, 2, T)[0:TQ]
        d_pt = B(13120, 2, NQ, TQ)[0:TQ]
        d_lam = B(13120, 4, DA_D)
        d_dg = B(14180, 3, TQ)[0:TQ]
        d_sq = B(14180 + 3 * TQ, T)
        on = fra[:, FR1:FR1 + 8 * T].rearrange("p (s k t) -> p s k t", s=2, k=4)
        O_COL = 2 * TQ

        def du(u):
            h = u // NQ
            return h, h // 2, h % 2, QS[u % NQ]

        def at_norm(s):
            return (s - 8) // NQ if s >= 8 and (s - 8) % NQ == 0 else None

        def pe_side(pe, s, slot):
            for kind, f, n, g, t, b, lag in side.get((s, slot), ()):
                if f + 1 > lag:
                    pe.wait_ge(s_da_fe, f + 1 - lag)
                if kind in "qkz":
                    wait_split(pe, n)
                    pe_proj(pe, 5, n, t, b, T)
                elif kind == "v":
                    wait_split(pe, n)
                    w_ = wview(n, KD, 256)
                    for k in range(KD):
                        mm = mm3(pe, ps[0:QS[t], b, 0:256], hsp(k, TQ * t, TQ * t + QS[t]), [x[:, k, :] for x in w_],
                                 k == 0, k == KD - 1)
                    mm.then_inc(s_tile, 1)
                elif kind == "r":
                    pe.wait_ge(s_da_fe, side_at[("qk"[t // 2], g, t % 2)] + 1)
                    for h in range(2):
                        mm = pe.matmul(ps[:, b + h, 0:HALF], cst[:, C_R128:C_R128 + P],
                                       d_raw[:, t, HALF * h:HALF * h + HALF], start=True, stop=True)
                    mm.then_inc(s_da_rq, 1)
                elif kind == "s":
                    pe.wait_ge(s_da_sq, 2 * g + t + 1)
                    for h in range(2):
                        mm = pe.matmul(ps[:, b + h, 0:HALF], cst[:, C_O128:C_O128 + P], d_sq[:, HALF * h:HALF * h + HALF],
                                       start=True, stop=True)
                    mm.then_inc(s_da_ss, 1)
                else:
                    wait_split(pe, n)
                    w_ = wview(n, 4, 512)
                    q = t % 4
                    for bb, t0, t1 in pieces(T):
                        for k in range(4):
                            pe.wait_ge(s_da_ol, 4 * (g // 2) + k + 1)
                            mm = mm3(pe, ps[:, b + bb, 0:HALF], [v[:, k, P * q:P * q + P] for v in w_],
                                     [on[:, x, k, t0:t1] for x in range(2)], k == 0, k == 3)
                    mm.then_inc(s_tile, 1)

        def pe_da(pe):
            pe.wait_ge(s_norm_rt, 6)
            pe_side(pe, -1, 0)
            for s in range(DA_STEPS):
                if s < DA_UNITS:
                    h, g, m, r = du(s)
                    i = s % NQ
                    if i == 0:
                        pe.wait_ge(s_da_qf, 2 * (h + 1))
                    for p in range(2):
                        if s > 0:
                            pe.wait_ge(s_da_ex, 2 * (s - 1) + p + 1)
                        for hf in range(2):
                            mm = pe.matmul(ps[0:r, 2 * p + hf, 0:HALF], d_qf[64 * p:64 * p + 64, m, TQ * i:TQ * i + r],
                                           d_qf[64 * p:64 * p + 64, 2 + m, HALF * hf:HALF * hf + HALF],
                                           start=True, stop=True)
                        mm.then_inc(s_da_s, 1)
                pe_side(pe, s, 0)
                u = s - 3
                if 0 <= u < DA_UNITS:
                    _, g, m, r = du(u)
                    pe.wait_ge(s_da_pa, u + 1)
                    pe.wait_ge(s_da_pb, u + 1)
                    if u % (2 * NQ) == 0:
                        pe.wait_ge(s_da_fe, side_at[("v", g, NQ - 1)] + 1)
                    for kt in range(NQ):
                        mm = pe.matmul(ps[:, 5, O_COL:O_COL + r], d_v[g % 2][0:QS[kt], kt, P * m:P * m + P],
                                       d_pt[0:QS[kt], u % 2, kt, 0:r], start=(kt == 0), stop=(kt == NQ - 1))
                    mm.then_inc(s_da_pv, 1)
                pe_side(pe, s, 1)
                u = s - 2
                if 0 <= u < DA_UNITS:
                    r = du(u)[3]
                    pe.wait_ge(s_da_cb, u + 1)
                    pe.wait_ge(s_da_dg, u + 1)
                    if u > 0:
                        pe.wait_ge(s_da_o, u)
                    for kt in range(NQ):
                        mm = pe.matmul(ps[0:QS[kt], 4 + kt // 3, TQ * (kt % 3):TQ * (kt % 3) + r],
                                       d_p[0:r, u % 3, 0, TQ * kt:TQ * kt + QS[kt]], d_dg[0:r, u % 3, 0:r],
                                       start=True, stop=True)
                    mm.then_inc(s_da_pt, 1)
                pe_side(pe, s, 2)

        def act_side(e, s, slot):
            for kind, f, n, g, t, b, lag in side.get((s, slot), ()):
                if kind == "s":
                    e.wait_ge(s_da_ss, 2 * g + t + 1)
                    e.activation(two(d_sq, T), bank(b, T), ACT.Sqrt, bias=cst[:, C_EPS5:C_EPS5 + 1]).then_inc(s_da_fe, 1)
                elif kind != "r":
                    if opens_chunk(kind, t):
                        act_split(e, split_no[n] + 1)
                    if kind in "qk":
                        wait_tile(e, n, t)
                        if g > 0:
                            e.wait_ge(s_da_qf, 2 * (2 * g - 1 + t))
                        e.activation(two(d_raw[:, 2 * (kind == "k") + t, :], T), bank(b, T), ACT.Copy,
                                     scale=float(DA_D) ** -0.5 if kind == "q" else 1.0).then_inc(s_da_fe, 1)
                    elif kind == "v":
                        wait_tile(e, n, t)
                        if g >= 2:
                            e.wait_ge(s_da_pv, 2 * NQ * (g - 1))
                        e.activation(d_v[g % 2][0:QS[t], t, :], ps[0:QS[t], b, 0:256], ACT.Copy).then_inc(s_da_fe, 1)
                    elif kind == "z":
                        wait_tile(e, n, t)
                        if g > 0:
                            e.wait_ge(s_da_oz, 2 * g - 1 + t)
                        e.activation(two(d_z[:, t, :], T), bank(b, T), ACT.Silu).then_inc(s_da_fe, 1)

        def act_da(e):
            e.dma_start(d_tab.rearrange("p a b -> p (a b)"), cc["rope"]).then_inc(s_tab_in, 16)
            e.dma_start(d_lam.rearrange("p a b -> p (a b)"),
                        cc["da_lambda_2"].rearrange("o a b -> o (a b)").partition_broadcast(P)).then_inc(s_tab_in, 16)
            e.wait_ge(s_lam_s, 2)
            e.activation(stat[:, 14:16], stat[:, 12:14], ACT.Exp).then_inc(s_lam_e, 1)
            act_side(e, -1, 0)
            for s in range(DA_STEPS):
                if s < DA_UNITS:
                    r = du(s)[3]
                    for p in range(2):
                        e.wait_ge(s_da_mx, 2 * s + p + 1)
                        if s >= 3:
                            e.wait_ge(s_da_pt, s - 2)
                            e.wait_ge(s_da_cb, s - 2)
                            e.wait_ge(s_da_dg, s - 2)
                        i = 2 * (s % 3) + p
                        e.activation(d_p[0:r, s % 3, p, :].rearrange("p (a b) -> p a b", a=2),
                                     ps[0:r, 2 * p:2 * p + 2, 0:HALF], ACT.Exp, bias=stat[0:r, 16 + i:17 + i],
                                     accum_out=stat[0:r, 22 + i:23 + i]).then_inc(s_da_ex, 1)
                h = at_norm(s)
                if h is not None:
                    e.wait_ge(s_da_o, NQ * (h + 1))
                    if h > 0:
                        e.wait_ge(s_da_on, h)
                    e.activation(d_sq, d_o[:, h % 2, :], ACT.Square).then_inc(s_da_sq, 1)
                act_side(e, s, 0)
                u = s - 3
                if 0 <= u < DA_UNITS:
                    h, _, m, r = du(u)
                    i = u % NQ
                    e.wait_ge(s_da_pv, u + 1)
                    if h >= 2:
                        e.wait_ge(s_da_oh, h - 1)
                        e.wait_ge(s_da_ol, h - 1)
                    e.activation(d_o[:, m, TQ * i:TQ * i + r], ps[:, 5, O_COL:O_COL + r], ACT.Copy).then_inc(s_da_o, 1)
                act_side(e, s, 1)
                u = s - 2
                if 0 <= u < DA_UNITS:
                    r = du(u)[3]
                    e.wait_ge(s_da_pt, u + 1)
                    if u >= 2:
                        e.wait_ge(s_da_pv, u - 1)
                    e.activation(d_pt[:, u % 2, 0:3, 0:r], ps[0:TQ, 4, 0:3 * TQ].rearrange("p (k c) -> p k c", k=3)[:, :, 0:r],
                                 ACT.Copy).then_inc(s_da_pa, 1)
                act_side(e, s, 2)
                h = at_norm(s - 1)
                if h is not None:
                    e.wait_ge(s_da_oz, h + 1)
                    if h >= 4:
                        e.wait_ge(s_tile, tiles_to[side_n[("o", h // 4 * 2 - 1)]])
                    e.activation(on[:, 0, h % 4, :], d_o[:, h % 2, :], ACT.Copy).then_inc(s_da_oh, 1)

        def pool_side(e, s, slot):
            for kind, f, n, g, t, b, lag in side.get((s, slot), ()):
                if kind == "r":
                    i = side_r[(g, t)]
                    e.wait_ge(s_da_rq, i + 1)
                    e.tensor_tensor(d_raw[:, t, :], d_raw[:, t, :], d_tab[:, 0, :], ALU.mult).then_inc(s_da_t1, 1)
                    e.wait_ge(s_da_t1, i + 1)
                    e.wait_ge(s_da_fe, f + 1)
                    e.tensor_tensor(d_qf[:, t, :], d_qf[:, t, :], d_raw[:, t, :], ALU.add).then_inc(s_da_qf, 1)
                elif kind != "s" and opens_chunk(kind, t):
                    pool_split(e, split_no[n] + 1)

        def pool_da(e):
            e.wait_ge(s_tab_in, 64)
            pool_side(e, -1, 0)
            for s in range(DA_STEPS):
                pool_side(e, s, 0)
                pool_side(e, s, 1)
                pool_side(e, s, 2)
                h = at_norm(s - 1)
                if h is not None:
                    e.wait_ge(s_da_oh, h + 1)
                    e.tensor_tensor(on[:, 1, h % 4, :], d_o[:, h % 2, :], on[:, 0, h % 4, :], ALU.subtract).then_inc(s_da_ol, 1)

        def dve_side(e, s, slot):
            for kind, f, n, g, t, b, lag in side.get((s, slot), ()):
                if kind == "r":
                    h = 2 * g + t % 2
                    e.wait_ge(s_da_rq, side_r[(g, t)] + 1)
                    if h >= 2:
                        e.wait_ge(s_da_s, 2 * NQ * (h - 1))
                    e.tensor_tensor(two(d_qf[:, t, :], T), bank(b, T), two(d_tab[:, 1, :], T), ALU.mult).then_inc(s_da_fe, 1)
                elif kind == "o":
                    wait_tile(e, n, t % 4)
                    y2 = two(hF[:, t, :], T)
                    if g > 1:
                        e.wait_ge(s_da_fe, side_at[("o", g - 2, t)] + 1)
                        e.tensor_tensor(y2, y2, bank(b, T), ALU.add).then_inc(s_da_fe, 1)
                    else:
                        e.tensor_copy(y2, bank(b, T)).then_inc(s_da_fe, 1)

        def dve_da(e):
            c = dve_chain
            e.wait_ge(s_tab_in, 64)
            for i in range(2):
                e.tensor_tensor_reduce(d_qf[:, i, 0:DA_D], d_lam[:, 2 * i, :], d_lam[:, 2 * i + 1, :], 1.0, 0.0,
                                       ALU.mult, ALU.add, stat[:, 12 + i:13 + i]).then_inc(s_lam_s, 1)
            e.wait_ge(s_lam_s, 2)
            e.wait_ge(s_lam_e, 1)
            c(e.tensor_tensor(stat[:, 12:13], stat[:, 15:16], stat[:, 14:15], ALU.subtract))
            c(e.tensor_scalar(col[:, G_LAM:G_LAM + 1], stat[:, 12:13], LAM_INIT, None, ALU.subtract))
            c(e.tensor_scalar(col[:, G_T:G_T + 1], col[:, G_SUB:G_SUB + 1], 1.0 - LAM_INIT, None, ALU.mult))
            dve_side(e, -1, 0)
            for s in range(DA_STEPS):
                if s < DA_UNITS:
                    r = du(s)[3]
                    for p in range(2):
                        e.wait_ge(s_da_s, 2 * s + p + 1)
                        i = 2 * (s % 3) + p
                        if s >= 3:
                            e.wait_ge(s_da_ex, 2 * (s - 2))
                        e.tensor_reduce(stat[0:r, 16 + i:17 + i], ps[0:r, 2 * p:2 * p + 2, 0:HALF], AX_XY, ALU.max,
                                        negate=True).then_inc(s_da_mx, 1)
                u = s - 1
                if 0 <= u < DA_UNITS:
                    r, i = du(u)[3], 2 * (u % 3)
                    e.wait_ge(s_da_ex, 2 * u + 2)
                    c(e.reciprocal(stat[0:r, 28 + i:30 + i], stat[0:r, 22 + i:24 + i]))
                    c(e.scalar_tensor_tensor(out=stat[0:r, 34 + i:35 + i], in0=stat[0:r, 22 + i:23 + i],
                                             scalar=col[0:r, G_LAM:G_LAM + 1], in1=stat[0:r, 29 + i:30 + i],
                                             op0=ALU.mult, op1=ALU.mult))
                    if u >= 3:
                        e.wait_ge(s_da_pt, u - 2)
                    e.tensor_scalar(d_dg[0:r, u % 3, 0:r], cst[0:r, C_ID:C_ID + r], stat[0:r, 28 + i:29 + i], None,
                                    ALU.mult).then_inc(s_da_dg, 1)
                    e.scalar_tensor_tensor(out=d_p[0:r, u % 3, 0, :], in0=d_p[0:r, u % 3, 1, :],
                                           scalar=stat[0:r, 34 + i:35 + i], in1=d_p[0:r, u % 3, 0, :],
                                           op0=ALU.mult, op1=ALU.add).then_inc(s_da_cb, 1)
                dve_side(e, s, 0)
                dve_side(e, s, 1)
                u = s - 2
                if 0 <= u < DA_UNITS:
                    r = du(u)[3]
                    e.wait_ge(s_da_pt, u + 1)
                    if u >= 2:
                        e.wait_ge(s_da_pv, u - 1)
                    for kt in (3, 4):
                        ins = e.tensor_copy(d_pt[0:QS[kt], u % 2, kt, 0:r], ps[0:QS[kt], 5, TQ * (kt - 3):TQ * (kt - 3) + r])
                    ins.then_inc(s_da_pb, 1)
                dve_side(e, s, 2)
                h = at_norm(s - 1)
                if h is not None:
                    m = h % 2
                    e.wait_ge(s_da_fe, side_at[("s", h // 2, m)] + 1)
                    c(e.reciprocal(d_sq, d_sq))
                    e.scalar_tensor_tensor(out=d_o[:, m, :], in0=d_o[:, m, :], scalar=col[:, G_T:G_T + 1], in1=d_sq,
                                           op0=ALU.mult, op1=ALU.mult).then_inc(s_da_on, 1)
                    e.wait_ge(s_da_on, h + 1)
                    e.wait_ge(s_da_fe, side_at[("z", h // 2, m)] + 1)
                    e.tensor_tensor(d_o[:, m, :], d_o[:, m, :], d_z[:, m, :], ALU.mult).then_inc(s_da_oz, 1)

        o_sb = B(0, 2, D)

        def pe_final(pe, need):
            for i in range(4):
                for hf in range(2):
                    j = 2 * i + hf
                    pe.wait_ge(s_x_done, need)
                    if j - 3 > 0:
                        pe.wait_ge(s_y_evac, j - 3)
                    for k in range(4):
                        m = pe.transpose(ps[:, j % 4, P * k:P * k + P],
                                         xT[:, 4 * hf + k, META + P * i:META + P * i + P], ident)
                    m.then_inc(s_y_t, 1)

        def act_final(e, need):
            e.wait_ge(s_x_done, need)
            for i in range(4):
                for hf in range(2):
                    j = 2 * i + hf
                    e.wait_ge(s_y_t, j + 1)
                    if i >= 2:
                        e.wait_ge(s_y_out[i % 2], 16 * (i // 2))
                    e.activation(o_sb[:, i % 2, 512 * hf:512 * hf + 512], ps[:, j % 4, :], ACT.Copy).then_inc(s_y_evac, 1)

        def sp_final(e):
            for i in range(4):
                e.wait_ge(s_y_evac, 2 * i + 2)
                e.dma_start(out[0, P * i:P * i + P, :], o_sb[:, i % 2, :]).then_inc(s_y_out[i % 2], 16)
            for b in range(2):
                e.wait_ge(s_y_out[b], 32)

        need = XD[5] + KD
        sp_extra = {mla_in[0] + RAW: sp_mla}

        block = ctx.enter_context(nc.Block())

        @block.sync
        def _(sp):
            sp_setup(sp)
            sp_weights(sp)
            sp_final(sp)

        @block.tensor
        def _(pe):
            pe_setup(pe)
            pe_filter_mlp(pe)
            pe_ada(pe)
            pe_norm(pe, 0)
            pe_fox(pe)
            pe_out(pe, 0, fox_out)
            pe_norm(pe, 1)
            pe_moe(pe, 0)
            pe_norm(pe, 2)
            pe_mla(pe)
            pe_out(pe, 1, mla_out)
            pe_norm(pe, 3)
            pe_moe(pe, 1)
            pe_norm(pe, 4)
            pe_hyena(pe)
            pe_post(pe, 0)
            pe_norm(pe, 5)
            pe_da(pe)
            pe_post(pe, 1)
            pe_final(pe, need)

        @block.scalar
        def _(act):
            nonlocal act_chain
            act_chain = Chain(act, s_act_chain)
            act_loads(act)
            act_setup(act)
            act_filter_loads(act)
            act_filter_mlp(act)
            act_filter_table(act)
            act_filter_abs(act, 0)
            filter_group_loads(act, 1)
            for g in range(HY_G):
                if g < HY_G - 1:
                    act_filter_abs(act, g + 1)
                if g < HY_G - 2:
                    filter_group_loads(act, g + 2)
                act_filter_store(act, g)
            act_norm(act, 0)
            act_split(act, 0)
            act_fox(act)
            act_out(act, 0, fox_out)
            act_norm(act, 1)
            act_moe(act, 0)
            act_norm(act, 2)
            act_mla(act)
            act_out(act, 1, mla_out)
            act_norm(act, 3)
            act_moe(act, 1)
            act_norm(act, 4)
            act_hyena(act)
            act_post(act, 0)
            act_norm(act, 5)
            act_da(act)
            act_post(act, 1)
            act_final(act, need)

        @block.gpsimd
        def _(pool):
            for g in range(HY_G):
                pool_filter_group(pool, g)
            pool_norm(pool, 0)
            pool_split(pool, 0)
            pool_fox(pool)
            pool_out(pool, 0, fox_out)
            pool_norm(pool, 1)
            pool_moe(pool, 0)
            pool_norm(pool, 2)
            pool_mla(pool)
            pool_out(pool, 1, mla_out)
            pool_norm(pool, 3)
            pool_moe(pool, 1)
            pool_norm(pool, 4)
            pool_hyena(pool)
            pool_norm(pool, 5)
            pool_da(pool)

        @block.vector
        def _(dve):
            nonlocal dve_chain
            dve_chain = Chain(dve, s_dve_chain)
            dve_setup(dve)
            dve_ada_chunks(dve, 0, 1)
            dve_filter_mlp(dve)
            dve_ada_chunks(dve, 1, ada_to(-1))
            dve_filter_table(dve)
            dve_filter_group(dve, 0)
            for g in range(HY_G):
                if g < HY_G - 1:
                    dve_filter_group(dve, g + 1)
                dve_ada_chunks(dve, ada_to(g - 1), ada_to(g))
            dve_filter_norm(dve)
            dve_ada(dve)
            dve_norm(dve, 0)
            dve_fox(dve)
            dve_out(dve, 0, fox_out)
            dve_norm(dve, 1)
            dve_moe(dve, 0)
            dve_norm(dve, 2)
            dve_mla(dve)
            dve_out(dve, 1, mla_out)
            dve_norm(dve, 3)
            dve_moe(dve, 1)
            dve_norm(dve, 4)
            dve_hyena(dve)
            dve_post(dve, 0)
            dve_norm(dve, 5)
            dve_da(dve)
            dve_post(dve, 1)


_INS = ["x", "c", "positions", "w_ada", "b_ada", "mix_norm", "ffn_norm", "fox_w_in", "fox_b_f", "fox_q_norm",
        "fox_k_norm", "fox_w_out", "mla_w_in", "mla_q_lat_norm", "mla_kv_lat_norm", "mla_w_uq", "mla_w_ukv",
        "mla_q_norm", "mla_k_norm", "mla_w_out", "moe_w_grp", "moe_b_grp", "moe_w_rt", "moe_b_rt", "moe_w_gate",
        "moe_w_up", "moe_w_down", "meta_2", "norm_pre_2", "norm_post_2", "hy_w_in_2", "hy_b_in_2", "hy_conv_w_2",
        "hy_conv_b_2", "hy_f_w1_2", "hy_f_b1_2", "hy_f_w2_2", "hy_f_b2_2", "hy_f_w3_2", "hy_f_b3_2", "hy_f_w4_2",
        "hy_f_freq_2", "hy_skip_2", "hy_w_out_2", "da_w_in_2", "da_lambda_2", "da_subln_2", "da_w_out_2"]


def kernel(**inputs):
    import concourse.bacc as bacc
    from concourse.bass_utils import run_bass_kernel_spmd

    nc = bacc.Bacc("TRN2", target_bir_lowering=False, num_devices=1)
    arrays, args = {}, {}
    data = {name: np.ascontiguousarray(inputs[name]) for name in _INS}
    data.update(constants())
    for name, v in data.items():
        arrays[f"in_{name}"] = v
        args[name] = nc.dram_tensor(f"in_{name}", v.shape, mybir.dt.from_np(v.dtype), kind="ExternalInput").ap()
    out = nc.dram_tensor("out_0", (1, SEQ, D), F32, kind="ExternalOutput").ap()
    build(nc, args, out)
    r = run_bass_kernel_spmd(nc, [arrays], core_ids=[0])
    return r.results[0]["out_0"]
```
